# Optimizing a Trainium2 kernel written in Bass

```python
import functools
import jax, jax.numpy as jnp
from jax import lax
import numpy as np

D_MODEL = 1024
BATCH = 1
SEQ = 512
DEPTH = 1
DEC_BATCH = 8
DEC_SEQ = 8
PAST_LEN = 2048
PAGE_SIZE = 128

A_GROUPS = ((128, 1), (512, 4), (2048, 16))
A_N_GROUPS = 3
A_HEADS = 8
A_HEAD_DIM = 64
A_WIDTH = A_HEADS * A_HEAD_DIM
A_STEPS = 128
A_BLOCK = 128
B_CHUNK = 128
B_GROUPS = 8
B_WIDTH = D_MODEL
B_GROUP_DIM = B_WIDTH // B_GROUPS
MOE_GROUPS = 4
MOE_EXPERTS_PER_GROUP = 4
MOE_EXPERTS = MOE_GROUPS * MOE_EXPERTS_PER_GROUP
MOE_TOP_K = 2
MOE_HIDDEN = 512
EPS = 1e-6
IN_COLS = 3 * A_N_GROUPS * A_WIDTH + 2 * B_WIDTH + 2 * D_MODEL

kernel_name = 'hybrid_dilated_attn_sgu_hmoe_step'

'''One decoder layer (DEPTH layers) of a hybrid decoder, applied to a prompt group and a sample group that share weights.

Layer:  h = adaLN-RMSNorm(x; c)
        [q,k,v | u,v | gA,gB] = h @ w_in (one combined projection)
        A = dilated ALiBi attention, 3 head groups (128,1),(512,4),(2048,16), group outputs combined per head slot
            with weights proportional to their softmax denominators (exp of log-sum-exp)
        B = gelu(u) * (tril(W_s) LN(gelu(v)) + b), per 128-position chunk, 8 channel groups
        x = x + gate1(c) * ((sig(gA) * A @ w_pa + sig(gB) * B @ w_pb) @ w_o)
        x = x + gate2(c) * HierMoE(adaLN-RMSNorm(x; c))   (top-1 group, then top-2 experts in it)
        y = adaLN-RMSNorm(x; c_final)
Inputs:
  x_prompt (BATCH, SEQ, D_MODEL) positions 0..SEQ-1; x_sample (DEC_BATCH, DEC_SEQ, D_MODEL) positions PAST_LEN..PAST_LEN+DEC_SEQ-1
  cache_kv_w128 / w512 / w2048 (DEPTH, DEC_BATCH, min(W, PAST_LEN), 2, A_HEADS, A_HEAD_DIM): K (index 0) and V (index 1)
      of the last min(W, PAST_LEN) positions for each dilation group
  c_prompt (BATCH, D_MODEL), c_sample (DEC_BATCH, D_MODEL); weights with a leading DEPTH axis; final-norm weights.
Outputs (tuple):
  y_prompt (BATCH, SEQ, D_MODEL), y_sample (DEC_BATCH, DEC_SEQ, D_MODEL),
  new_kv_w128_prompt, new_kv_w512_prompt, new_kv_w2048_prompt: (DEPTH, BATCH, min(W, SEQ), 2, A_HEADS, A_HEAD_DIM)
  new_kv_w128_sample, new_kv_w512_sample, new_kv_w2048_sample: (DEPTH, DEC_BATCH, DEC_SEQ, 2, A_HEADS, A_HEAD_DIM)
  new_sgu_v_sample: (DEPTH, DEC_BATCH, DEC_SEQ, B_WIDTH) normalised v rows opening the chunk at PAST_LEN
'''

def alibi_slopes():
    n = A_N_GROUPS * A_HEADS
    e = jnp.arange(1, n + 1, dtype=jnp.float32)
    return jnp.exp2(-8.0 * e / n).reshape(A_N_GROUPS, A_HEADS)

def adaln(c, w, b, n):
    mod = jax.nn.silu(c) @ w + b
    return jnp.split(mod, n, axis=-1)

def rmsnorm_mod(x, gain, shift, scale):
    xf = x.astype(jnp.float32)
    y = xf * lax.rsqrt(jnp.mean(jnp.square(xf), axis=-1, keepdims=True) + EPS)
    y = y * gain.astype(jnp.float32) * (1.0 + scale[:, None, :].astype(jnp.float32)) + shift[:, None, :].astype(jnp.float32)
    return y.astype(x.dtype)

def layernorm(x, g, b):
    xf = x.astype(jnp.float32)
    mu = jnp.mean(xf, axis=-1, keepdims=True)
    var = jnp.mean(jnp.square(xf - mu), axis=-1, keepdims=True)
    return ((xf - mu) * lax.rsqrt(var + EPS) * g.astype(jnp.float32) + b.astype(jnp.float32)).astype(x.dtype)

def in_projection(h, w_in):
    z = h @ w_in
    b, s, _ = z.shape
    n_qkv = 3 * A_N_GROUPS * A_WIDTH
    qkv = z[..., :n_qkv].reshape(b, s, 3, A_N_GROUPS, A_HEADS, A_HEAD_DIM)
    o = n_qkv
    u = jax.nn.gelu(z[..., o:o + B_WIDTH])
    v = jax.nn.gelu(z[..., o + B_WIDTH:o + 2 * B_WIDTH])
    o = o + 2 * B_WIDTH
    ga = jax.nn.sigmoid(z[..., o:o + D_MODEL])
    gb = jax.nn.sigmoid(z[..., o + D_MODEL:o + 2 * D_MODEL])
    return qkv, u, v, ga, gb

def dilated_attn_prompt(q, k, v, dil, slopes):
    b, s, h, dh = q.shape
    n_steps = s // dil
    nb = -(-n_steps // A_BLOCK)
    pad = nb * A_BLOCK - n_steps

    def to_blocks(t):
        t = t.reshape(b, n_steps, dil, h, dh)
        t = jnp.pad(t, ((0, 0), (0, pad), (0, 0), (0, 0), (0, 0)))
        return t.reshape(b, nb, A_BLOCK, dil, h, dh)

    def with_prev(t):
        prev = jnp.pad(t[:, :-1], ((0, 0), (1, 0), (0, 0), (0, 0), (0, 0), (0, 0)))
        return jnp.concatenate([prev, t], axis=2)

    qb = to_blocks(q)
    kc = with_prev(to_blocks(k))
    vc = with_prev(to_blocks(v))
    scores = jnp.einsum('bnqrhd,bnkrhd->bnrhqk', qb, kc, preferred_element_type=jnp.float32) * (dh ** -0.5)
    qi = jnp.arange(A_BLOCK)[:, None]
    ki = jnp.arange(2 * A_BLOCK)[None, :]
    delta = qi + A_BLOCK - ki
    band = (delta >= 0) & (delta <= A_STEPS)
    has_prev = (jnp.arange(nb) > 0)[:, None, None] | (ki >= A_BLOCK)[None]
    valid = band[None] & has_prev
    dist = (delta * dil).astype(jnp.float32)
    scores = scores - slopes[:, None, None] * dist[None]
    scores = jnp.where(valid[None, :, None, None], scores, -jnp.inf)
    m = jnp.max(scores, axis=-1, keepdims=True)
    p = jnp.exp(scores - m)
    den = jnp.sum(p, axis=-1)
    o = jnp.einsum('bnrhqk,bnkrhd->bnqrhd', p, vc.astype(jnp.float32))
    den = jnp.transpose(den, (0, 1, 4, 2, 3))
    lse = jnp.transpose(m[..., 0], (0, 1, 4, 2, 3)) + jnp.log(den)
    o = o / den[..., None]
    o = o.reshape(b, nb * A_BLOCK, dil, h, dh)[:, :n_steps].reshape(b, s, h, dh)
    lse = lse.reshape(b, nb * A_BLOCK, dil, h)[:, :n_steps].reshape(b, s, h)
    return o, lse

def dilated_attn_sample(q, k_new, v_new, k_buf, v_buf, dil, slopes):
    buf, t, dh = k_buf.shape[1], q.shape[1], q.shape[-1]
    kc = jnp.concatenate([k_buf, k_new.astype(k_buf.dtype)], axis=1)
    vc = jnp.concatenate([v_buf, v_new.astype(v_buf.dtype)], axis=1)
    j = jnp.arange(A_STEPS + 1)
    idx = buf + jnp.arange(t)[:, None] - dil * j[None, :]
    valid = idx >= 0
    idx = jnp.maximum(idx, 0)
    kg = kc[:, idx]
    vg = vc[:, idx]
    scores = jnp.einsum('bthd,btjhd->bhtj', q, kg, preferred_element_type=jnp.float32) * (dh ** -0.5)
    scores = scores - slopes[:, None, None] * (dil * j).astype(jnp.float32)[None, None, :]
    scores = jnp.where(valid[None, None], scores, -jnp.inf)
    m = jnp.max(scores, axis=-1, keepdims=True)
    p = jnp.exp(scores - m)
    den = jnp.sum(p, axis=-1)
    o = jnp.einsum('bhtj,btjhd->bthd', p, vg.astype(jnp.float32)) / jnp.transpose(den, (0, 2, 1))[..., None]
    lse = jnp.transpose(m[..., 0] + jnp.log(den), (0, 2, 1))
    return o, lse

def combine_groups(outs, lses):
    w = jax.nn.softmax(jnp.stack(lses, axis=0), axis=0)
    return jnp.sum(w[..., None] * jnp.stack(outs, axis=0), axis=0)

def mixer_a_prompt(qkv, slopes):
    outs, lses, new_kv = [], [], []
    for g, (win, dil) in enumerate(A_GROUPS):
        q, k, v = qkv[:, :, 0, g], qkv[:, :, 1, g], qkv[:, :, 2, g]
        o, lse = dilated_attn_prompt(q, k, v, dil, slopes[g])
        outs.append(o)
        lses.append(lse)
        keep = min(win, q.shape[1])
        new_kv.append(jnp.stack([k[:, -keep:], v[:, -keep:]], axis=2))
    return combine_groups(outs, lses), new_kv

def mixer_a_sample(qkv, caches, slopes):
    outs, lses, new_kv = [], [], []
    for g, (win, dil) in enumerate(A_GROUPS):
        q, k, v = qkv[:, :, 0, g], qkv[:, :, 1, g], qkv[:, :, 2, g]
        kv_buf = caches[g]
        o, lse = dilated_attn_sample(q, k, v, kv_buf[:, :, 0], kv_buf[:, :, 1], dil, slopes[g])
        outs.append(o)
        lses.append(lse)
        new_kv.append(jnp.stack([k, v], axis=2))
    return combine_groups(outs, lses), new_kv

def spatial_gating(u, v, w_s, b_s):
    b, s, _ = v.shape
    cl = min(s, B_CHUNK)
    vb = v.reshape(b, s // cl, cl, B_GROUPS, B_GROUP_DIM)
    w = jnp.where(jnp.tril(jnp.ones((cl, cl), dtype=bool)), w_s[:, :cl, :cl], 0.0)
    mixed = jnp.einsum('gts,bnsgc->bntgc', w, vb) + jnp.transpose(b_s[:, :cl])[None, None, :, :, None]
    return u * mixed.reshape(b, s, B_WIDTH).astype(u.dtype)

def hier_moe(h, w_rg, b_rg, w_re, b_re, w_gate, w_up, w_down):
    b, s, d = h.shape
    x = h.reshape(b * s, d)
    g_logits = (x @ w_rg + b_rg).astype(jnp.float32)
    g_prob, g_idx = lax.top_k(jax.nn.softmax(g_logits, axis=-1), 1)
    e_logits = (jnp.einsum('nd,gde->nge', x, w_re) + b_re).astype(jnp.float32)
    e_logits = jnp.take_along_axis(e_logits, g_idx[:, :, None], axis=1)[:, 0]
    e_top, e_idx = lax.top_k(e_logits, MOE_TOP_K)
    weights = jax.nn.softmax(e_top, axis=-1) * g_prob
    expert = g_idx * MOE_EXPERTS_PER_GROUP + e_idx
    combine = jnp.einsum('nk,nke->ne', weights, jax.nn.one_hot(expert, MOE_EXPERTS, dtype=jnp.float32))
    hg = jnp.einsum('nd,edf->nef', x, w_gate)
    hu = jnp.einsum('nd,edf->nef', x, w_up)
    act = (jax.nn.silu(hg) * hu).astype(jnp.float32) * combine[:, :, None]
    y = jnp.einsum('nef,efd->nd', act.astype(x.dtype), w_down)
    return y.reshape(b, s, d)

def decoder_layer(x, c, attend, w_ada, b_ada, norm1_g, norm2_g, w_in, sgu_ln_g, sgu_ln_b, sgu_w, sgu_b,
                  w_pa, w_pb, w_o, w_rg, b_rg, w_re, b_re, w_gate, w_up, w_down):
    sh1, sc1, gt1, sh2, sc2, gt2 = adaln(c, w_ada, b_ada, 6)
    h = rmsnorm_mod(x, norm1_g, sh1, sc1)
    qkv, u, v, ga, gb = in_projection(h, w_in)
    o_a, new_kv = attend(qkv)
    vn = layernorm(v, sgu_ln_g, sgu_ln_b)
    o_b = spatial_gating(u, vn, sgu_w, sgu_b)
    b, s = x.shape[:2]
    pa = o_a.reshape(b, s, A_WIDTH).astype(x.dtype) @ w_pa
    pb = o_b @ w_pb
    x = x + gt1[:, None, :] * ((ga * pa + gb * pb) @ w_o)
    h = rmsnorm_mod(x, norm2_g, sh2, sc2)
    x = x + gt2[:, None, :] * hier_moe(h, w_rg, b_rg, w_re, b_re, w_gate, w_up, w_down)
    return x, new_kv, vn

def setup_inputs(seed: int = 0) -> dict:
    key = jax.random.key(seed)
    ks = iter(jax.random.split(key, 40))

    def nrm(shape, scale):
        return jax.random.normal(next(ks), shape, jnp.float32) * scale

    L, D = DEPTH, D_MODEL
    x_prompt = nrm((BATCH, SEQ, D), 1.0)
    x_sample = nrm((DEC_BATCH, DEC_SEQ, D), 1.0)
    cache_kv_w128 = nrm((L, DEC_BATCH, min(A_GROUPS[0][0], PAST_LEN), 2, A_HEADS, A_HEAD_DIM), 1.0)
    cache_kv_w512 = nrm((L, DEC_BATCH, min(A_GROUPS[1][0], PAST_LEN), 2, A_HEADS, A_HEAD_DIM), 1.0)
    cache_kv_w2048 = nrm((L, DEC_BATCH, min(A_GROUPS[2][0], PAST_LEN), 2, A_HEADS, A_HEAD_DIM), 1.0)
    c_prompt = nrm((BATCH, D), 1.0)
    c_sample = nrm((DEC_BATCH, D), 1.0)
    return {
        'x_prompt': x_prompt,
        'x_sample': x_sample,
        'cache_kv_w128': cache_kv_w128,
        'cache_kv_w512': cache_kv_w512,
        'cache_kv_w2048': cache_kv_w2048,
        'c_prompt': c_prompt,
        'c_sample': c_sample,
        'w_ada': nrm((L, D, 6 * D), 0.5 * D ** -0.5),
        'b_ada': nrm((L, 6 * D), 0.02),
        'norm1_g': 1.0 + nrm((L, D), 0.05),
        'norm2_g': 1.0 + nrm((L, D), 0.05),
        'w_in': nrm((L, D, IN_COLS), D ** -0.5),
        'sgu_ln_g': 1.0 + nrm((L, B_WIDTH), 0.05),
        'sgu_ln_b': nrm((L, B_WIDTH), 0.02),
        'sgu_w': jnp.tril(nrm((L, B_GROUPS, B_CHUNK, B_CHUNK), B_CHUNK ** -0.5)),
        'sgu_b': 1.0 + nrm((L, B_GROUPS, B_CHUNK), 0.1),
        'w_pa': nrm((L, A_WIDTH, D), A_WIDTH ** -0.5),
        'w_pb': nrm((L, B_WIDTH, D), B_WIDTH ** -0.5),
        'w_o': nrm((L, D, D), D ** -0.5),
        'w_route_group': nrm((L, D, MOE_GROUPS), D ** -0.5),
        'b_route_group': nrm((L, MOE_GROUPS), 0.01),
        'w_route_expert': nrm((L, MOE_GROUPS, D, MOE_EXPERTS_PER_GROUP), D ** -0.5),
        'b_route_expert': nrm((L, MOE_GROUPS, MOE_EXPERTS_PER_GROUP), 0.01),
        'w_gate': nrm((L, MOE_EXPERTS, D, MOE_HIDDEN), D ** -0.5),
        'w_up': nrm((L, MOE_EXPERTS, D, MOE_HIDDEN), D ** -0.5),
        'w_down': nrm((L, MOE_EXPERTS, MOE_HIDDEN, D), MOE_HIDDEN ** -0.5),
        'normf_g': 1.0 + nrm((D,), 0.05),
        'w_ada_final': nrm((D, 2 * D), 0.5 * D ** -0.5),
        'b_ada_final': nrm((2 * D,), 0.02),
    }

def reference(x_prompt, x_sample, cache_kv_w128, cache_kv_w512, cache_kv_w2048, c_prompt, c_sample,
              w_ada, b_ada, norm1_g, norm2_g, w_in, sgu_ln_g, sgu_ln_b, sgu_w, sgu_b, w_pa, w_pb, w_o,
              w_route_group, b_route_group, w_route_expert, b_route_expert, w_gate, w_up, w_down,
              normf_g, w_ada_final, b_ada_final):
    slopes = alibi_slopes()
    hp, hs = x_prompt, x_sample
    kv_p = ([], [], [])
    kv_s = ([], [], [])
    v_s = []
    for l in range(DEPTH):
        lw = (w_ada[l], b_ada[l], norm1_g[l], norm2_g[l], w_in[l], sgu_ln_g[l], sgu_ln_b[l], sgu_w[l], sgu_b[l],
              w_pa[l], w_pb[l], w_o[l], w_route_group[l], b_route_group[l], w_route_expert[l], b_route_expert[l],
              w_gate[l], w_up[l], w_down[l])
        attend_p = functools.partial(mixer_a_prompt, slopes=slopes)
        hp, new_p, _ = decoder_layer(hp, c_prompt, attend_p, *lw)
        attend_s = functools.partial(mixer_a_sample,
                                     caches=(cache_kv_w128[l], cache_kv_w512[l], cache_kv_w2048[l]),
                                     slopes=slopes)
        hs, new_s, vn_s = decoder_layer(hs, c_sample, attend_s, *lw)
        for g in range(A_N_GROUPS):
            kv_p[g].append(new_p[g])
            kv_s[g].append(new_s[g])
        v_s.append(vn_s)
    shp, scp = adaln(c_prompt, w_ada_final, b_ada_final, 2)
    y_prompt = rmsnorm_mod(hp, normf_g, shp, scp)
    shs, scs = adaln(c_sample, w_ada_final, b_ada_final, 2)
    y_sample = rmsnorm_mod(hs, normf_g, shs, scs)
    new_kv_w128_prompt = jnp.stack(kv_p[0], axis=0)
    new_kv_w512_prompt = jnp.stack(kv_p[1], axis=0)
    new_kv_w2048_prompt = jnp.stack(kv_p[2], axis=0)
    new_kv_w128_sample = jnp.stack(kv_s[0], axis=0)
    new_kv_w512_sample = jnp.stack(kv_s[1], axis=0)
    new_kv_w2048_sample = jnp.stack(kv_s[2], axis=0)
    new_sgu_v_sample = jnp.stack(v_s, axis=0)
    return (y_prompt, y_sample, new_kv_w128_prompt, new_kv_w512_prompt, new_kv_w2048_prompt,
            new_kv_w128_sample, new_kv_w512_sample, new_kv_w2048_sample, new_sgu_v_sample)


_drawn_inputs = setup_inputs


def setup_inputs(seed=0):
    import zlib

    import numpy as np

    out = dict(_drawn_inputs(seed))
    spreads = {}
    factors = {'cache_kv_w128': 5.943,
     'cache_kv_w512': 2.905,
     'norm2_g': 3.394,
     'sgu_ln_b': 2.753,
     'sgu_b': 4.274,
     'b_route_group': 8.0,
     'b_route_expert': 8.0,
     'cache_kv_w2048': 4.329}
    for name, (base, spread) in spreads.items():
        noise = np.random.default_rng([zlib.crc32(name.encode()), seed]).standard_normal(out[name].shape)
        drawn = base * np.exp(spread * noise) if base else spread * noise
        out[name] = __import__('jax').numpy.asarray(drawn.astype(out[name].dtype))
    for name, factor in factors.items():
        out[name] = (out[name] * factor).astype(out[name].dtype)
    return out
```

```python
from contextlib import ExitStack

import numpy as np

import concourse.bass as bass
from concourse import mybir

F32 = mybir.dt.float32
U32 = mybir.dt.uint32
ALU = mybir.AluOpType
ACT = mybir.ActivationFunctionType
AX = mybir.AxisListType

P = 128
D = 1024
KD = D // P
SEQ, NB, NT = 512, 8, 8
NS = NB * NT
TILES = 5
ROWS = [P] * 4 + [NS]
TOK = SEQ + NS
H, DH = 8, 64
AW = H * DH
DILS = (1, 4, 16)
WINS = (128, 512, 2048)
STEPS = 128
CH = 512
E_ALL, FF = 16, 512
CAP = 128
EROWS = 640
EPS = 1e-6
NEG = -1e30
SLOTS = 4
SLOT = 4096
NC_CLS = (1, 4, 8)
CLS0 = (0, 1, 5)
XT = 13
KEYS = STEPS + NS
OW = AW + 16


def head_of(hp):
    return 2 * (hp % 4) + hp // 4


CST = {}


def const_layout():
    at = 0
    for name, width in (("ident", P), ("tril", P), ("before", P), ("ones", P), ("dmask", AW), ("seltok", NT),
                        ("selmod", P + NS), ("rep", NS), ("blk", NB), ("iota", 16), ("ebase", 16),
                        ("blkt", NS), ("valid", TILES)):
        CST[name] = (at, at + width)
        at += width
    return at


CONST_W = const_layout()


def slopes():
    n = 24
    return np.exp2(-8.0 * np.arange(1, n + 1, dtype=np.float32) / np.float32(n)).reshape(3, 8).astype(np.float32)


def constants():
    c = np.zeros((P, CONST_W), np.float32)

    def put(name, rows, a):
        c[:rows, CST[name][0]:CST[name][1]] = a

    i = np.arange(P)
    put("ident", P, np.eye(P))
    put("tril", P, i[:, None] <= i[None, :])
    put("before", P, i[:, None] < i[None, :])
    put("ones", P, 1.0)
    r = np.arange(NS)
    put("dmask", NS, (r % H)[:, None] == np.arange(AW)[None, :] // DH)
    put("seltok", NS, (r // H)[:, None] == np.arange(NT)[None, :])
    sel = np.zeros((9, P + NS))
    sel[0, :P] = 1
    sel[1 + r // NT, P + r] = 1
    put("selmod", 9, sel)
    put("rep", NT, np.arange(NT)[:, None] == (r % NT)[None, :])
    put("blk", NS, (r // NT)[:, None] == np.arange(NB)[None, :])
    put("blkt", NS, (r // NT)[:, None] == (r // NT)[None, :])
    put("iota", P, np.arange(16)[None, :])
    put("ebase", P, np.arange(16)[None, :] * EROWS)
    put("valid", P, (i[:, None] + P * np.arange(TILES)[None, :]) < TOK)
    return c


def empty_slots():
    row = np.arange(E_ALL * EROWS + CAP, dtype=np.uint32)
    return np.stack([0 * row, 2 * TOK + row % CAP], axis=1).astype(np.uint32)


def token_places():
    tok = np.arange(P)[:, None] + P * np.arange(TILES)[None, :]
    a = np.stack([np.stack([tok, 2 * tok + k], axis=-1) for k in range(2)], axis=1)
    return a.reshape(P, 4 * TILES).astype(np.uint32)


def prompt_bias():
    s = slopes()
    q, k = np.arange(P)[:, None], np.arange(P)[None, :]
    out = np.full((4, P, H, P), NEG, np.float32)
    for kind, g, dist, ok in ((0, 0, q + P - k, k >= q), (1, 0, q - k, k <= q), (2, 1, 4 * (q - k), k <= q),
                              (3, 2, 4 * (q - k), (k <= q) & ((q - k) % 4 == 0))):
        dist = dist.astype(np.float32)
        for hp in range(H):
            out[kind, :, hp][ok] = -(s[g, head_of(hp)] * dist)[ok]
    return out


def sample_bias():
    s = slopes()
    out = np.full((NB, NS, 3, KEYS), NEG, np.float32)
    for g, dil in enumerate(DILS):
        for t in range(NT):
            for h in range(H):
                row = t * H + h
                c = np.arange(STEPS)
                j = (t + WINS[g] - (c * dil + t % dil)) // dil
                ok = (j >= 0) & (j <= STEPS)
                out[:, row, g, :STEPS][:, ok] = -(s[g, h] * (dil * j).astype(np.float32))[ok]
                for n in range(t + 1):
                    if (t - n) % dil == 0:
                        for b in range(NB):
                            out[b, row, g, STEPS + b * NT + n] = -(s[g, h] * np.float32(t - n))
    return out


def copy_keys(tp, KT, kt_read):
    def copy(eng, unit, b, x):
        u, n = tp.first[f"kt{b}"] + x, XT * b + x
        if n >= 3:
            eng.wait_ge(kt_read, n - 2)
        tp.wait_filled(eng, u)
        src = tp.bank(u).rearrange("p (k n) -> p k n", k=4)
        if tp.users[u] == "act":
            unit.activation(KT[:, n % 3, :, :], src, ACT.Copy).then_inc(tp.done(u), 1)
        else:
            unit.tensor_copy(KT[:, n % 3, :, :], src).then_inc(tp.done(u), 1)

    return copy


class Ring:

    def __init__(self, banks, filled, emptied_act, emptied_dve):
        self.banks, self.filled = banks, filled
        self.emptied = {"act": emptied_act, "dve": emptied_dve}
        self.users, self.first = [], {}

    def stage(self, name, uses, user):
        self.first[name] = len(self.users)
        self.users += [user] * uses

    def bank(self, m):
        return self.banks[m % len(self.banks)]

    def wait_empty(self, pe, m):
        if m >= len(self.banks):
            self.wait_emptied(pe, m - len(self.banks))

    def wait_emptied(self, eng, m):
        user = self.users[m]
        eng.wait_ge(self.emptied[user], self.users[:m + 1].count(user))

    def wait_filled(self, eng, m):
        eng.wait_ge(self.filled, m + 1)

    def done(self, m):
        return self.emptied[self.users[m]]


def build(nc, t, out):
    ctx = ExitStack()
    with ctx:
        def sem(name):
            return ctx.enter_context(nc.semaphore(name))

        def dram(name, shape, dt=F32):
            return nc.dram_tensor(name, shape, dt, kind="Internal").ap()

        cst = ctx.enter_context(nc.sbuf_tensor("cst", [P, CONST_W], F32))
        stat = ctx.enter_context(nc.sbuf_tensor("stat", [P, 672], F32))
        kept = ctx.enter_context(nc.sbuf_tensor("kept", [P, 768 * 2 + 1536 + 2304], F32))
        ring_w = SLOTS * SLOT
        HT0, MIX0 = ring_w, ring_w + KD * TOK
        WK0 = MIX0 + TILES * D
        WORK = 19640
        main = ctx.enter_context(nc.sbuf_tensor("main", [P, WK0 + WORK], F32))
        psum = ctx.enter_context(nc.psum_tensor("psum", [P, 8, CH], F32))

        def c_(name, rows=P):
            a, b = CST[name]
            return cst[0:rows, a:b]

        def at(start, *shape):
            n = int(np.prod(shape))
            v = main[:, start:start + n]
            if len(shape) == 2:
                v = v.rearrange("p (a b) -> p a b", a=shape[0])
            elif len(shape) == 3:
                v = v.rearrange("p (a b c) -> p a b c", a=shape[0], b=shape[1])
            elif len(shape) == 4:
                v = v.rearrange("p (a b c d) -> p a b c d", a=shape[0], b=shape[1], c=shape[2])
            return v

        def slot(n):
            return at((n % SLOTS) * SLOT, SLOT)

        def wslot(n):
            return at((n % SLOTS) * SLOT, KD, CH)

        hT = at(HT0, KD, TOK)
        mix = at(MIX0, TILES, D)
        qTs = kept[:, 0:768].rearrange("p (g j n) -> p g j n", g=3, j=4)
        kTs = kept[:, 768:1536].rearrange("p (g j n) -> p g j n", g=3, j=4)
        vs = kept[:, 1536:3072].rearrange("p (g n) -> p g n", g=3)
        oT = kept[:, 3072:5376].rearrange("p (j n) -> p j n", j=4)
        mod = at(WK0, 3, 2, D)
        gain = at(WK0 + 6144, D)
        x0 = at(WK0 + 7168, TILES, D)
        obT = at(WK0 + 12288, KD, TOK)
        crow = at(WK0 + 12288, D)
        modrow = at(WK0 + 13312, 2, CH)
        modbias = at(WK0 + 14336, 2, CH)
        junk = at(WK0 + 15360, D)
        sguw = at(WK0 + 16896, H, P)
        sguT = at(WK0 + 17920, H, P)
        sguTs = at(WK0 + 18944, H, NS)
        lng = mod[:, 2, 0, :]
        lnb = mod[:, 2, 1, :]
        qn = at(WK0, TILES, CH)
        kn = at(WK0 + 2560, TILES, CH)
        vn = at(WK0 + 5120, 4, CH)
        qT = at(WK0 + 7168, 4, SEQ)
        kT = at(WK0 + 9216, 4, SEQ)
        sc = at(WK0 + 11264, H, 2 * P)
        pT = at(WK0 + 13312, 2, H, P)
        abias = at(WK0 + 15360, 2, H, P)
        oe = at(WK0 + 17408, 2, OW)
        oin = at(WK0, 4, 3 * OW)
        oc = at(WK0 + 6400, 2, AW)
        KT = at(WK0, 3, 4, P)
        om = at(WK0 + 1536, AW)
        pTn = at(WK0 + 2048, 3, NS)
        ssc = at(WK0 + 2304, 2, 3, KEYS)
        pTm = at(WK0 + 3456, 14 * NS)
        Qm = at(WK0 + 7424, 2, 15 * 256 + 16)
        sbias = at(WK0 + 18464, 2, 3, KEYS)
        sga = at(WK0 + 7168, TILES, D)
        x1 = sga
        mixT = obT
        modrow2 = at(WK0 + 16896, 2, CH)
        modbias2 = at(WK0 + 17920, 2, CH)
        gt_tmp = at(WK0 + 18944, CH)
        hrow = at(WK0 + 12288, 2, D)
        h2T = hT
        wrt = stat[:, 340:500].rearrange("p (k n) -> p k n", k=KD)
        brt = stat[:, 312:332]
        snm, sden, sf = (stat[:, 512 + 6 * n:518 + 6 * n].rearrange("p (b g) -> p b g", b=2) for n in range(3))
        smin = stat[:, 530:532]
        gp, w1, w2 = (stat[:, 540 + 5 * n:545 + 5 * n] for n in range(3))
        rounds_f = stat[:, 560:561]
        rounds_u = stat[:, 561:562].bitcast(U32)
        tok_u = stat[:, 600:620].bitcast(U32).rearrange("p (k i a) -> p k i a", k=2, i=TILES)
        row_u = stat[:, 570:580].bitcast(U32).rearrange("p (k i) -> p k i", k=2)
        slot_u = stat[:, 580:584].bitcast(U32).rearrange("p (b n) -> p b n", b=2)
        dest_u = stat[:, 584:588].bitcast(U32).rearrange("p (b n) -> p b n", b=2)
        RT0 = WK0 + 14336

        def rt(start, *shape):
            return at(RT0 + start, *shape)

        lg, eg = rt(0, TILES, 20), rt(100, TILES, 4)
        eq4, cand4, on_g, on_1, on_2 = (rt(120 + 20 * n, TILES, 4) for n in range(5))
        esel, esel2 = rt(220, TILES, 4), rt(240, TILES, 4)
        sc5, id5, e1m, e2m = (rt(260 + 5 * n, TILES) for n in range(4))
        pick, m1, m2, mask, place = (rt(280 + 80 * n, TILES, 16) for n in range(5))
        rowf = rt(680, 2, TILES)
        tmp5 = rt(690, TILES, 4, 4)
        ring6 = [at(n * SLOT, SLOT) for n in range(6)]
        xg = at(WK0 + 12288, 2, D)
        yb = at(WK0 + 14336, 2, D)
        xgT = kept[:, 0:2048].rearrange("p (b k n) -> p b k n", b=2, k=KD)
        sg = kept[:, 2048:3072].rearrange("p (b n) -> p b n", b=2)
        ac = kept[:, 3072:4096].rearrange("p (b n) -> p b n", b=2)
        acT = kept[:, 4096:5120].rearrange("p (b k n) -> p b k n", b=2, k=4)
        yg = at(0, 2, 2, D)
        yt = at(4096, 2, D)
        cT = stat[:, 0:72].rearrange("p (k n) -> p k n", k=KD)
        sgubT, sgubTs = stat[:, 136:144], stat[:, 144:152]
        ss, rs, lnr = stat[:, 152:157], stat[:, 160:165], stat[:, 168:173]
        bns = stat[:, 176:236].rearrange("p (i n) -> p i n", i=TILES)
        mv = stat[:, 240:250].rearrange("p (i n) -> p i n", i=TILES)
        nmin = stat[:, 256:264]
        fw = stat[:, 264:288].rearrange("p (g h) -> p g h", g=3)
        fd = stat[:, 288:312].rearrange("p (g h) -> p g h", g=3)
        KV_OUTS = [4, 4 + 10, 4 + 10 + 10]

        const_in, x_in, c_in = sem("const_in"), sem("x_in"), sem("c_in")
        slot_in = [sem(f"slot_in{i}") for i in range(SLOTS)]
        mm_filled, mm_act, mm_dve = sem("mm_filled"), sem("mm_act"), sem("mm_dve")
        tp_filled, tp_act, tp_dve = sem("tp_filled"), sem("tp_act"), sem("tp_dve")
        act_step, dve_step, pool_step = sem("act_step"), sem("dve_step"), sem("pool_step")
        silu_done = sem("silu_done")
        bias_in = [sem(f"bias_in{i}") for i in range(2)]
        o_out = [sem(f"o_out{i}") for i in range(2)]
        stat_set = sem("stat_set")
        gain_in, sq_done, var_done, sqrt_done, hn_done = (sem(n) for n in (
            "gain_in", "sq_done", "var_done", "sqrt_done", "hn_done"))
        sgu_in, ln_in, lnvar, lnsqrt, vn_done, vout = (sem(n) for n in (
            "sgu_in", "ln_in", "lnvar", "lnsqrt", "vn_done", "vout"))
        sb_in = [sem(f"sb_in{i}") for i in range(2)]
        q_spread, kt_read, s_max, s_exp, p_ready = (sem(n) for n in (
            "q_spread", "kt_read", "s_max", "s_exp", "p_ready"))
        def pair(name):
            return [sem(f"{name}{n}") for n in range(2)]

        gate_in, up_in, down_in = pair("gate_in"), pair("up_in"), pair("down_in")
        idx_in, xg_in, dest_in = pair("idx_in"), pair("xg_in"), pair("dest_in")
        xt0_filled, xt1_filled, gate_filled, up_filled, at_filled, y0_filled, down_filled = (pair(n) for n in (
            "xt0_filled", "xt1_filled", "gate_filled", "up_filled", "at_filled", "y0_filled", "down_filled"))
        xt_act, xt_dve, sg_done, ac_done, at_done, y_act, y_dve, y_out = (pair(n) for n in (
            "xt_act", "xt_dve", "sg_done", "ac_done", "at_done", "y_act", "y_dve", "y_out"))
        sq3, var3, sqrt3, y_done, y_final = (sem(n) for n in ("sq3", "var3", "sqrt3", "y_done", "y_final"))
        yg_in2 = pair("yg_in")
        x2_done = sem("x2_done")
        pool_turn = sem("pool_turn")
        x1_in, x1_done, h2_done, rt_in, rt_exp_in, rt_exp, mask_done, rows_done, zero_out, tok_out = (
            sem(n) for n in ("x1_in", "x1_done", "h2_done", "rt_in", "rt_exp_in", "rt_exp", "mask_done", "rows_done",
                             "zero_out", "tok_out"))
        sq2, var2, sqrt2 = sem("sq2"), sem("var2"), sem("sqrt2")
        h2_out = [sem(f"h2_out{i}") for i in range(2)]
        kv_out, abias_in, scored, exped, oin_in, lse_dif, lse_exp, oc_done = (
            sem(n) for n in ("kv_out", "abias_in", "scored", "exped",
                             "oin_in", "lse_dif", "lse_exp", "oc_done"))

        mm = Ring([psum[:, b, :] for b in range(6)], mm_filled, mm_act, mm_dve)
        tp = Ring([psum[:, b, :] for b in (6, 7)], tp_filled, tp_act, tp_dve)
        tp.stage("c", 1, "dve")
        mm.stage("ada1", 4 * 3, "dve")
        tp.stage("h", 2 * TILES, "act")
        mm.stage("v", 2 * TILES, "act")
        tp.stage("sgu", 3, "dve")
        tp.stage("rep", 1, "dve")
        mm.stage("u", 2 * TILES, "act")
        mm.stage("sgu", 2 * TILES, "dve")
        tp.stage("ob", 2 * TILES, "act")
        mm.stage("gb", 2 * TILES, "act")
        mm.stage("pb", 2 * TILES, "dve")
        GT = [(g, i, [i - 1, i] if g == 0 and i else [i]) for g in range(3) for i in range(4)]
        for g in range(3):
            mm.stage(f"q{g}", TILES, "act")
            mm.stage(f"k{g}", TILES, "dve")
            mm.stage(f"w{g}", TILES, "act")
            tp.stage(f"qk{g}", 2 * TILES, "act")
            for _, i, keys in GT[4 * g:4 * g + 4]:
                mm.stage(f"s{g}{i}", 2 * len(keys), "dve")
                tp.stage(f"p{g}{i}", 2 * len(keys), "act")
                mm.stage(f"o{g}{i}", 1, "dve")
        tp.stage("o", 4, "act")
        KT_USER = ["act", "dve"] * 6 + ["act"]
        for b in range(NB + 2):
            if b < NB:
                tp.first[f"kt{b}"] = len(tp.users)
                tp.users += KT_USER
                mm.stage(f"ss{b}", 3, "dve")
            if b >= 2:
                tp.stage(f"ot{b - 2}", 1, "act")
            if 1 <= b <= NB:
                tp.stage(f"pt{b - 1}", 1, "dve")
                mm.stage(f"so{b - 1}", 1, "dve")
        mm.stage("ga", 2 * TILES, "act")
        mm.stage("pa", 2 * TILES, "dve")
        mm.stage("ada2", 6 * 3, "dve")
        tp.stage("mix", 2 * TILES, "act")
        mm.stage("wo", 2 * TILES, "dve")
        tp.stage("h2", 2 * TILES, "act")
        mm.stage("rt", TILES, "dve")
        mm.stage("ada3", 6 * 3, "dve")
        tp.stage("pos", 1, "dve")

        h2d = dram("h2d", (TOK, D))
        yd = dram("yd", (2 * TOK + CAP, D))
        slots_d = dram("slots_d", (E_ALL * EROWS + CAP, 2), U32)
        oscr = [dram(f"oscr{g}", (SEQ, OW)) for g in range(3)]

        def chunk(w, j):
            return w.rearrange("(k p) n -> p k n", p=P)[:, :, j * CH:(j + 1) * CH]

        w_in, w_ada, w_adaf = t["w_in"][0], t["w_ada"][0], t["w_ada_final"]
        ada = [(w_ada, t["b_ada"][0], j) for j in range(12)] + [(w_adaf, t["b_ada_final"], j) for j in range(4)]
        QKV = 3 * 3 * AW
        stream, S0 = [], {}

        slot_last = []

        def put(name, last, *srcs):
            S0[name] = len(stream)
            stream.extend(srcs)
            slot_last.extend(last)

        def fifth(name, n):
            return [mm.first[name] + TILES * j + TILES - 1 for j in range(n)]

        put("ada1", [mm.first["ada1"] + 3 * n for n in range(4)], *[chunk(ada[j][0], ada[j][2]) for j in range(4)])
        put("v", fifth("v", 2), *[chunk(w_in, QKV // CH + 2 + j) for j in range(2)])
        put("u", fifth("u", 2), *[chunk(w_in, QKV // CH + j) for j in range(2)])
        put("gb", fifth("gb", 2), *[chunk(w_in, QKV // CH + 6 + j) for j in range(2)])
        put("pb", fifth("pb", 2), *[chunk(t["w_pb"][0], j) for j in range(2)])
        for g in range(3):
            put(f"qkv{g}", [fifth(f"{x}{g}", 1)[0] for x in "qkw"], *[chunk(w_in, 3 * j + g) for j in range(3)])
        caches = [t[f"cache_kv_w{w}"][0] for w in WINS]

        def keys_of(b, kv, g):
            c = caches[g][b].rearrange("(c r) kv h d -> c r kv (h d)", r=DILS[g])
            return c[:, 0:NC_CLS[g], kv, :]

        def kv_slots(b, kv, last):
            put(f"{'KV'[kv]}{b}", last, [(slice(0, 1), keys_of(b, kv, 0)), (slice(1, 5), keys_of(b, kv, 1))],
                [(slice(0, 8), keys_of(b, kv, 2))])

        for b in range(NB + 1):
            if b < NB:
                f = mm.first[f"ss{b}"]
                kv_slots(b, 0, [f + 1, f + 2])
            if b:
                kv_slots(b - 1, 1, [mm.first[f"so{b - 1}"]] * 2)
        put("ga", fifth("ga", 2), *[chunk(w_in, QKV // CH + 4 + j) for j in range(2)])
        put("pa", [mm.first["pa"] + 9], t["w_pa"][0].rearrange("(j p) n -> p j n", p=P))
        put("ada2", [mm.first["ada2"] + 3 * n for n in range(6)], *[chunk(ada[j][0], ada[j][2]) for j in range(4, 10)])
        put("wo", fifth("wo", 2), *[chunk(t["w_o"][0], j) for j in range(2)])
        put("ada3", [mm.first["ada3"] + 3 * n for n in range(6)], *[chunk(ada[j][0], ada[j][2]) for j in range(10, 16)])
        N_SLOTS = len(stream)
        slot_total, totals = [], [0] * SLOTS
        for n, src in enumerate(stream):
            totals[n % SLOTS] += 16 * (len(src) if isinstance(src, list) else 1)
            slot_total.append(totals[n % SLOTS])

        def perm(ap, g, i):
            if g == 0:
                return ap[:, i * P:(i + 1) * P]
            return ap[:, i:SEQ:4]

        def rows_of(ap, g, i):
            return ap[i * P:(i + 1) * P] if g == 0 else ap.rearrange("(s r) n -> r s n", r=4)[i]

        PAIRS = E_ALL // 2

        def rounds_of(eng):
            tp.wait_emptied(eng, tp.first["pos"])
            return eng.value_load(rounds_u[0:1, 0:1], min_val=1, max_val=EROWS // CAP)

        def prime(eng, *pairs):
            for both in pairs:
                for s in both:
                    eng.sem_inc(s, 1)

        block = ctx.enter_context(nc.Block())

        @block.sync
        def _(sp):
            for n, src in enumerate(stream):
                if n >= SLOTS:
                    sp.wait_ge(mm_filled, slot_last[n - SLOTS] + 1)
                for part, a in src if isinstance(src, list) else [(slice(0, src.shape[1]), src)]:
                    dst = slot(n).rearrange("p (k n) -> p k n", n=a.shape[-1])[:, part, :]
                    sp.dma_start(dst, a).then_inc(slot_in[n % SLOTS], 16)
            rounds = rounds_of(sp)
            for n in range(N_SLOTS - SLOTS, N_SLOTS):
                sp.wait_ge(mm_filled, slot_last[n] + 1)
            with sp.Fori(0, rounds * PAIRS) as it:
                e = (it % PAIRS) * 2

                def weights(w, par, k):
                    return w[0][bass.ds(e + par, 1)].rearrange("a (k p) n -> p (a k) n", k=k)

                def load(par, n, w, k, free, into):
                    sp.wait_ge(free[par], it + 1)
                    sp.dma_start(ring6[3 * par + n].rearrange("p (k n) -> p k n", k=k),
                                 weights(w, par, k)).then_inc(into[par], 16)

                load(0, 0, t["w_gate"], KD, gate_filled, gate_in)
                load(0, 1, t["w_up"], KD, up_filled, up_in)
                load(1, 0, t["w_gate"], KD, gate_filled, gate_in)
                load(1, 1, t["w_up"], KD, up_filled, up_in)
                load(0, 2, t["w_down"], 4, down_filled, down_in)
                load(1, 2, t["w_down"], 4, down_filled, down_in)

        @block.gpsimd
        def _(pool):
            pool.dma_start(crow[0:1, :], t["c_prompt"]).then_inc(c_in, 16)
            pool.dma_start(crow[1:1 + NB, :], t["c_sample"]).then_inc(c_in, 16)
            pool.dma_start(cst[:, :], t["consts"]).then_inc(const_in, 16)
            pool.dma_start(x0[:, 0:4, :], t["x_prompt"][0].rearrange("(i p) d -> p i d", p=P)).then_inc(x_in, 16)
            pool.dma_start(x0[0:NS, 4, :], t["x_sample"].rearrange("b t d -> (b t) d")).then_inc(x_in, 16)
            pool.dma_start(gain, t["norm1_g"].partition_broadcast(P)).then_inc(gain_in, 16)
            def bias_rows(name, buf, j0, count):
                for n in range(count):
                    if n >= 2:
                        mm.wait_emptied(pool, mm.first[name] + 3 * (n - 2))
                    elif name == "ada3":
                        mm.wait_emptied(pool, mm.first["ada2"] + 3 * (4 + n))
                    _, b, j = ada[j0 + n]
                    pool.dma_start(buf[0:9, n % 2, :], b[j * CH:(j + 1) * CH].rearrange("(a n) -> a n", a=1)
                                   .partition_broadcast(9)).then_inc(bias_in[n % 2], 16)

            bias_rows("ada1", modbias, 0, 4)
            pool.dma_start(sguw, t["sgu_w"][0].rearrange("g t s -> t g s")).then_inc(sgu_in, 16)
            pool.dma_start(stat[0:H, 384:512], t["sgu_b"][0]).then_inc(sgu_in, 16)
            pool.dma_start(lng, t["sgu_ln_g"].partition_broadcast(P)).then_inc(ln_in, 16)
            pool.dma_start(lnb, t["sgu_ln_b"].partition_broadcast(P)).then_inc(ln_in, 16)
            pool.wait_ge(vn_done, TILES)
            pool.dma_start(out["sgu_v"], mix[0:NS, 4, :]).then_inc(vout, 16)
            for g in range(3):
                for kind in ((0, 1), (2,), (3,))[g]:
                    if kind < 2:
                        if kind == 0:
                            pool.wait_ge(mm_filled, mm.first["pb"] + 10)
                    else:
                        pool.wait_ge(scored, 4 * g)
                    pool.dma_start(abias[:, kind if kind < 2 else 1, :, :],
                                   t["pbias"][kind]).then_inc(abias_in, 16)
                mm.wait_emptied(pool, mm.first[f"k{g}"] + TILES - 1)
                mm.wait_emptied(pool, mm.first[f"w{g}"] + TILES - 1)
                kvp, kvs = out["kvp"][g], out["kvs"][g]
                for part, src in ((0, kn), (1, vn)):
                    for i in range(4):
                        if g == 0 and i < 3:
                            continue
                        rows = kvp if g == 0 else rows_of(kvp, g, i)
                        pool.dma_start(rows[:, part * AW:(part + 1) * AW], src[:, i, :]).then_inc(kv_out, 16)
                pool.dma_start(kvs[:, 0:AW], kn[0:NS, 4, :]).then_inc(kv_out, 16)
                pool.dma_start(kvs[:, AW:2 * AW], vs[0:NS, g, :]).then_inc(kv_out, 16)
                for i in range(4):
                    mm.wait_emptied(pool, mm.first[f"o{g}{i}"])
                    pool.dma_start(rows_of(oscr[g], g, i), oe[:, i % 2, :]).then_inc(o_out[i % 2], 16)
            for o in o_out:
                pool.wait_ge(o, 16 * 6)
            for g in range(3):
                pool.dma_start(oin[:, :, g * OW:(g + 1) * OW], oscr[g].rearrange("(i p) n -> p i n", p=P)).then_inc(oin_in, 16)
            for b in range(NB):
                if b >= 2:
                    mm.wait_emptied(pool, mm.first[f"ss{b - 2}"] + 2)
                pool.dma_start(sbias[0:NS, b % 2, :, :], t["sbias"][b]).then_inc(sb_in[b % 2], 16)
            mm.wait_emptied(pool, mm.first[f"ss{NB - 1}"] + 2)
            pool.dma_start(gain, t["norm2_g"].partition_broadcast(P)).then_inc(gain_in, 16)
            pool.dma_start(wrt[:, :, 0:4], t["w_route_group"][0].rearrange("(k p) n -> p k n", p=P)).then_inc(rt_in, 16)
            for g in range(4):
                pool.dma_start(wrt[:, :, 4 + 4 * g:8 + 4 * g],
                               t["w_route_expert"][0, g].rearrange("(k p) n -> p k n", p=P)).then_inc(rt_in, 16)
            pool.dma_start(brt[:, 0:4], t["b_route_group"].partition_broadcast(P)).then_inc(rt_in, 16)
            pool.dma_start(brt[:, 4:20], t["b_route_expert"].rearrange("a g e -> a (g e)").partition_broadcast(P)).then_inc(rt_in, 16)
            bias_rows("ada2", modbias2, 4, 6)
            mm.wait_emptied(pool, mm.first["pa"] + 9)
            pool.dma_start(x1[:, 0:4, :], t["x_prompt"][0].rearrange("(i p) d -> p i d", p=P)).then_inc(x1_in, 16)
            pool.dma_start(x1[0:NS, 4, :], t["x_sample"].rearrange("b t d -> (b t) d")).then_inc(x1_in, 16)
            for i in range(TILES):
                pool.wait_ge(h2_done, i + 1)
                pool.dma_start(h2d[i * P:i * P + ROWS[i], :], hrow[0:ROWS[i], i % 2, :]).then_inc(h2_out[i % 2], 16)
            mm.wait_emptied(pool, mm.first["ada2"] + 17)
            pool.dma_start(gain, t["normf_g"].rearrange("(a n) -> a n", a=1).partition_broadcast(P)).then_inc(gain_in, 16)
            bias_rows("ada3", modbias2, 10, 6)
            pool.dma_start(slots_d, t["empty_slots"]).then_inc(zero_out, 16)
            pool.dma_start(tok_u.rearrange("p k i a -> p (k i a)"), t["token_places"]).then_inc(zero_out, 16)
            pool.wait_ge(zero_out, 32)
            pool.wait_ge(rows_done, 1)
            for k in range(2):
                for i in range(TILES):
                    n = ROWS[i]
                    pool.indirect_dma_start(slots_d, bass.IndirectOffsetOnAxis(ap=row_u[0:n, k, i:i + 1], axis=0),
                                            tok_u[0:n, k, i, :], None).then_inc(tok_out, 16)
            pool.wait_ge(tok_out, 16 * 2 * TILES)
            for n in range(2):
                pool.wait_ge(h2_out[n], 16 * (3 - n))
            rounds = rounds_of(pool)

            def waited():
                pool.sem_inc(pool_turn, 1)

            def fetch(it, par, read):
                row = ((it % PAIRS) * 2 + par) * EROWS + (it // PAIRS) * CAP
                pool.dma_start(slot_u[:, par, :], slots_d[bass.ds(row, CAP), :]).then_inc(idx_in[par], 16)
                pool.wait_ge(idx_in[par], it * 16 + 16)
                if read is not None:
                    pool.wait_ge(xt1_filled[par], read)
                waited()
                pool.indirect_dma_start(xg[:, par, :], None, h2d, bass.IndirectOffsetOnAxis(
                    ap=slot_u[:, par, 0:1], axis=0)).then_inc(xg_in[par], 16)

            def scatter(it, par):
                row = ((it % PAIRS) * 2 + par) * EROWS + (it // PAIRS) * CAP
                pool.dma_start(dest_u[:, par, :], slots_d[bass.ds(row, CAP), :]).then_inc(dest_in[par], 16)
                pool.wait_ge(dest_in[par], it * 16 + 16)
                pool.wait_ge(y_act[par], it + 2)
                pool.wait_ge(y_dve[par], it + 2)
                pool.wait_ge(y_out[1 - par], it * 16 + 16 if par == 0 else it * 16 + 32)
                waited()
                pool.indirect_dma_start(yd, bass.IndirectOffsetOnAxis(ap=dest_u[:, par, 1:2], axis=0),
                                        yb[:, par, :], None).then_inc(y_out[par], 16)

            for par in range(2):
                pool.dma_start(yd[2 * TOK + par:2 * TOK + par + 1, :], h2d[par:par + 1, :]).then_inc(y_out[par], 16)
            fetch(0, 0, None)
            fetch(0, 1, None)
            with pool.Fori(0, rounds * PAIRS) as it:
                scatter(it, 0)
                for par in range(2):
                    pool.wait_ge(xg_in[par], it * 16 + 16)
                    fetch(it + 1, par, it + 1)
                scatter(it, 1)
            for par in range(2):
                pool.wait_ge(xg_in[par], rounds * (PAIRS * 16) + 16)
                pool.wait_ge(y_out[par], rounds * (PAIRS * 16) + 16)
            waited()
            for i in range(TILES):
                n = ROWS[i]
                if i >= 2:
                    pool.wait_ge(x2_done, i - 1)
                pool.dma_start(yg[0:n, i % 2, :, :], yd[2 * i * P:2 * (i * P + n), :].rearrange("(p k) n -> p k n", k=2)
                               ).then_inc(yg_in2[i % 2], 16)
            pool.wait_ge(kv_out, 16 * KV_OUTS[-1])
            pool.wait_ge(vout, 16)
            for i in range(TILES):
                pool.wait_ge(y_done, i + 1)
                dst = out["y_prompt"][i * P:(i + 1) * P, :] if i < 4 else out["y_sample"]
                pool.dma_start(dst, x1[0:ROWS[i], i, :]).then_inc(y_final, 16)
            pool.wait_ge(y_final, 16 * TILES)

        @block.tensor
        def _(pe):
            used = [0]

            def slot_wait(n):
                pe.wait_ge(slot_in[n % SLOTS], slot_total[n])

            def transposes(first, u, n, pieces):
                tp.wait_empty(pe, first + u)
                bank = tp.bank(first + u)
                for k, a in enumerate(pieces):
                    ins = nc.tensor.transpose(bank[0:a.shape[-1], k * n:k * n + a.shape[0]], a,
                                              c_("ident", a.shape[0])[:, 0:a.shape[0]])
                ins.then_inc(tp_filled, 1)

            def project(name, slotname, lhs, j, order=None, g=0):
                n = S0[slotname] + j
                slot_wait(n)
                for i in range(TILES):
                    m = mm.first[name] + (0 if order is None else order) + i
                    mm.wait_empty(pe, m)
                    for k in range(KD):
                        a = lhs[:, k, SEQ:TOK] if i == 4 else perm(lhs[:, k, :], g, i)
                        ins = nc.tensor.matmul(mm.bank(m)[0:ROWS[i], :], a, wslot(n)[:, k, :],
                                               start=(k == 0), stop=(k == KD - 1))
                    ins.then_inc(mm_filled, 1)

            def modulation(name, cT, rows, count):
                def row(n):
                    m = mm.first[name] + 3 * n
                    slot_wait(S0[name] + n)
                    mm.wait_empty(pe, m)
                    for k in range(KD):
                        ins = nc.tensor.matmul(mm.bank(m)[0:9, :], cT[:, k, :], wslot(S0[name] + n)[:, k, :],
                                               start=(k == 0), stop=(k == KD - 1))
                    ins.then_inc(mm_filled, 1)

                def spread(n):
                    mm.wait_emptied(pe, mm.first[name] + 3 * n)
                    for s in range(2):
                        m = mm.first[name] + 3 * n + 1 + s
                        mm.wait_empty(pe, m)
                        w = (P, NS)[s]
                        nc.tensor.matmul(mm.bank(m)[0:w, :], c_("selmod", 9)[:, s * P:s * P + w], rows[0:9, n % 2, :],
                                         start=True, stop=True).then_inc(mm_filled, 1)

                for n in range(count):
                    row(n)
                    spread(n)

            pe.wait_ge(const_in, 16)
            pe.wait_ge(silu_done, 1)
            transposes(tp.first["c"], 0, 9, [crow[0:9, k * P:(k + 1) * P] for k in range(KD)])
            tp.wait_emptied(pe, tp.first["c"])
            modulation("ada1", cT, modrow, 4)
            for i in range(TILES):
                pe.wait_ge(hn_done, i + 1)
                for half in range(2):
                    transposes(tp.first["h"], 2 * i + half, ROWS[i],
                               [x0[0:ROWS[i], i, (4 * half + k) * P:(4 * half + k + 1) * P] for k in range(4)])
            tp.wait_emptied(pe, tp.first["h"] + 2 * TILES - 1)
            for j in range(2):
                project("v", "v", hT, j, order=TILES * j)
            pe.wait_ge(sgu_in, 32)
            for half in range(2):
                transposes(tp.first["sgu"], half, P, [sguw[:, 4 * half + k, :] for k in range(4)])
            transposes(tp.first["sgu"], 2, H, [stat[0:H, 384:512]])
            tp.wait_emptied(pe, tp.first["sgu"] + 2)
            m = tp.first["rep"]
            tp.wait_empty(pe, m)
            nc.tensor.matmul(tp.bank(m)[0:NS, 0:NS], c_("rep", NT), sguT[0:NT, :, 0:NT], start=True, stop=True)
            nc.tensor.matmul(tp.bank(m)[0:NS, NS:NS + H], c_("rep", NT), sgubT[0:NT, :],
                             start=True, stop=True).then_inc(tp_filled, 1)
            for j in range(2):
                project("u", "u", hT, j, order=TILES * j)
            tp.wait_emptied(pe, tp.first["rep"])
            for i in range(TILES):
                pe.wait_ge(vn_done, i + 1)
                for half in range(2):
                    m = mm.first["sgu"] + 2 * i + half
                    mm.wait_empty(pe, m)
                    for k in range(4):
                        g = 4 * half + k
                        n = ROWS[i]
                        ins = nc.tensor.matmul(mm.bank(m)[0:n, k * P:(k + 1) * P],
                                               (sguT[:, g, :] if i < 4 else sguTs[0:NS, g, :]),
                                               mix[0:n, i, g * P:(g + 1) * P], start=True, stop=True)
                    ins.then_inc(mm_filled, 1)
            for i in range(TILES):
                mm.wait_emptied(pe, mm.first["sgu"] + 2 * i + 1)
                for half in range(2):
                    transposes(tp.first["ob"], 2 * i + half, ROWS[i],
                               [x0[0:ROWS[i], i, (4 * half + k) * P:(4 * half + k + 1) * P] for k in range(4)])
            for j in range(2):
                project("gb", "gb", hT, j, order=TILES * j)
            tp.wait_emptied(pe, tp.first["ob"] + 9)
            for j in range(2):
                project("pb", "pb", obT, j, order=TILES * j)
            for g in range(3):
                for j, name in enumerate(("q", "k", "w")):
                    project(f"{name}{g}", f"qkv{g}", hT, j, g=g)
                for j, src in enumerate((qn, kn)):
                    mm.wait_emptied(pe, mm.first[f"{'qk'[j]}{g}"] + TILES - 1)
                    for i in range(TILES):
                        transposes(tp.first[f"qk{g}"], TILES * j + i, ROWS[i],
                                   [src[0:ROWS[i], i, k * P:(k + 1) * P] for k in range(4)])
                tp.wait_emptied(pe, tp.first[f"qk{g}"] + 2 * TILES - 1)
                for _, i, keys in GT[4 * g:4 * g + 4]:
                    nk = len(keys)
                    for kk, kt in enumerate(keys):
                        for par in range(2):
                            m = mm.first[f"s{g}{i}"] + 2 * kk + par
                            mm.wait_empty(pe, m)
                            for j in range(4):
                                ins = nc.tensor.matmul(mm.bank(m)[:, j * P:(j + 1) * P],
                                                       qT[64 * par:64 * par + 64, j, i * P:(i + 1) * P],
                                                       kT[64 * par:64 * par + 64, j, kt * P:(kt + 1) * P],
                                                       start=True, stop=True)
                            ins.then_inc(mm_filled, 1)
                    pe.wait_ge(exped, 4 * g + i + 1)
                    for kk in range(nk):
                        for par in range(2):
                            transposes(tp.first[f"p{g}{i}"], 2 * kk + par, P,
                                       [sc[:, 4 * par + j, kk * P:(kk + 1) * P] for j in range(4)])
                    tp.wait_emptied(pe, tp.first[f"p{g}{i}"] + 2 * nk - 1)
                    if i == 0:
                        mm.wait_emptied(pe, mm.first[f"w{g}"] + TILES - 1)
                    m = mm.first[f"o{g}{i}"]
                    mm.wait_empty(pe, m)
                    for hp in range(H):
                        h = head_of(hp)
                        for kk, kt in enumerate(keys):
                            ins = nc.tensor.matmul(mm.bank(m)[:, h * DH:(h + 1) * DH], pT[:, kk, hp, :],
                                                   vn[:, kt, h * DH:(h + 1) * DH], start=(kk == 0), stop=(kk == nk - 1))
                    ins.then_inc(mm_filled, 1)
            for i in range(4):
                pe.wait_ge(oc_done, i + 1)
                transposes(tp.first["o"], i, P, [oc[:, i % 2, k * P:(k + 1) * P] for k in range(4)])

            def key_tile(b, x):
                n = S0[f"K{b}"] + (x >= CLS0[2])
                return slot(n).rearrange("p (k n) -> p k n", n=AW)[:, x - (CLS0[2] if x >= CLS0[2] else 0), :], n

            def turn_keys(b, x):
                tile, n = key_tile(b, x)
                if x in (0, CLS0[2]):
                    slot_wait(n)
                transposes(tp.first[f"kt{b}"], x, P, [tile[:, j * P:(j + 1) * P] for j in range(4)])

            def scores(b):
                pe.wait_ge(q_spread, b + 1)
                turn_keys(b, 0)
                for x in range(XT):
                    g = 0 if x < CLS0[1] else 1 if x < CLS0[2] else 2
                    if x + 1 < XT:
                        turn_keys(b, x + 1)
                    m = mm.first[f"ss{b}"] + g
                    if x == CLS0[g]:
                        mm.wait_empty(pe, m)
                    tp.wait_emptied(pe, tp.first[f"kt{b}"] + x)
                    for j in range(4):
                        ins = nc.tensor.matmul(mm.bank(m)[0:NS, 0:P], Qm[:, b % 2, x * 256 + j * NS:x * 256 + (j + 1) * NS],
                                               KT[:, (XT * b + x) % 3, j, :], start=(x == CLS0[g] and j == 0),
                                               stop=(x == CLS0[g] + NC_CLS[g] - 1 and j == 3))
                    ins.then_inc(kt_read, 1)
                    if x == CLS0[g] + NC_CLS[g] - 1:
                        whole = (0, 13, 14)[g]
                        for j in range(4):
                            ins = nc.tensor.matmul(mm.bank(m)[0:NS, P:KEYS],
                                                   Qm[:, b % 2, whole * 256 + j * NS:whole * 256 + (j + 1) * NS],
                                                   kTs[:, g, j, :], start=(j == 0), stop=(j == 3))
                        ins.then_inc(mm_filled, 1)

            def attend(b):
                u = tp.first[f"pt{b}"]
                pe.wait_ge(p_ready, b + 1)
                tp.wait_empty(pe, u)
                bank = tp.bank(u)
                for g in range(3):
                    nc.tensor.transpose(bank[:, g * NS:(g + 1) * NS], ssc[0:NS, b % 2, g, 0:P],
                                        c_("ident", NS)[:, 0:NS])
                for g in range(3):
                    ins = nc.tensor.transpose(bank[0:NS, (3 + g) * NS:(4 + g) * NS], ssc[0:NS, b % 2, g, P:KEYS],
                                              c_("ident", NS)[:, 0:NS])
                ins.then_inc(tp_filled, 1)
                m = mm.first[f"so{b}"]
                mm.wait_empty(pe, m)
                tp.wait_emptied(pe, u)
                for g in range(3):
                    nc.tensor.matmul(mm.bank(m)[0:NS, :], pTn[0:NS, g, :], vs[0:NS, g, :], start=(g == 0), stop=False)
                for x in range(XT):
                    n = S0[f"V{b}"] + (x >= CLS0[2])
                    if x in (0, CLS0[2]):
                        slot_wait(n)
                    tile = slot(n).rearrange("p (k n) -> p k n", n=AW)[:, x - (CLS0[2] if x >= CLS0[2] else 0), :]
                    ins = nc.tensor.matmul(mm.bank(m)[0:NS, :], pTm[:, x * NS:(x + 1) * NS], tile, start=False,
                                           stop=(x == XT - 1))
                ins.then_inc(mm_filled, 1)

            def gather_heads(b):
                u = tp.first[f"ot{b}"]
                mm.wait_emptied(pe, mm.first[f"so{b}"])
                tp.wait_empty(pe, u)
                for j in range(4):
                    ins = nc.tensor.matmul(tp.bank(u)[:, j * NT:(j + 1) * NT], om[0:NS, j * P:(j + 1) * P],
                                           c_("seltok", NS), start=True, stop=True)
                ins.then_inc(tp_filled, 1)

            for b in range(NB + 2):
                if b < NB:
                    scores(b)
                if b >= 2:
                    gather_heads(b - 2)
                if 1 <= b <= NB:
                    attend(b - 1)
            for j in range(2):
                project("ga", "ga", hT, j, order=TILES * j)
            slot_wait(S0["pa"])
            tp.wait_emptied(pe, tp.first[f"ot{NB - 1}"])
            wpa = slot(S0["pa"]).rearrange("p (j n) -> p j n", j=4)
            for c in range(2):
                for i in range(TILES):
                    m = mm.first["pa"] + TILES * c + i
                    mm.wait_empty(pe, m)
                    for j in range(4):
                        ins = nc.tensor.matmul(mm.bank(m)[0:ROWS[i], :], oT[:, j, i * P:i * P + ROWS[i]],
                                               wpa[:, j, c * CH:(c + 1) * CH], start=(j == 0), stop=(j == 3))
                    ins.then_inc(mm_filled, 1)
            modulation("ada2", cT, modrow2, 6)
            mm.wait_emptied(pe, mm.first["pa"] + 9)
            for i in range(TILES):
                for half in range(2):
                    transposes(tp.first["mix"], 2 * i + half, ROWS[i],
                               [mix[0:ROWS[i], i, (4 * half + k) * P:(4 * half + k + 1) * P] for k in range(4)])
            tp.wait_emptied(pe, tp.first["mix"] + 9)
            for j in range(2):
                project("wo", "wo", mixT, j, order=TILES * j)
            for i in range(TILES):
                pe.wait_ge(h2_done, i + 1)
                for half in range(2):
                    transposes(tp.first["h2"], 2 * i + half, ROWS[i],
                               [hrow[0:ROWS[i], i % 2, (4 * half + k) * P:(4 * half + k + 1) * P] for k in range(4)])
            pe.wait_ge(rt_in, 16 * 6)
            for i in range(TILES):
                m = mm.first["rt"] + i
                mm.wait_empty(pe, m)
                tp.wait_emptied(pe, tp.first["h2"] + 2 * i + 1)
                for k in range(KD):
                    ins = nc.tensor.matmul(mm.bank(m)[0:ROWS[i], 0:20], h2T[:, k, i * P:i * P + ROWS[i]], wrt[:, k, :],
                                           start=(k == 0), stop=(k == KD - 1))
                ins.then_inc(mm_filled, 1)
            modulation("ada3", cT, modrow2, 6)
            m = tp.first["pos"]
            pe.wait_ge(mask_done, 1)
            tp.wait_empty(pe, m)
            for i in range(TILES + 1):
                for e in range(min(i, TILES - 1) + 1 if i < TILES else TILES):
                    own_tile = e == i
                    last = e == min(i, TILES - 1)
                    ins = nc.tensor.matmul(tp.bank(m)[:, 16 * i:16 * i + 16], c_("before") if own_tile else c_("ones"),
                                           mask[:, e, :], start=(e == 0), stop=last)
            ins.then_inc(tp_filled, 1)
            rounds = rounds_of(pe)
            XTB, GATE, AT, Y = (psum[:, 0, :], psum[:, 1, :]), psum[:, 2, :], psum[:, 5, :], (psum[:, 6, :], psum[:, 7, :])
            UP = (psum[:, 3, :], psum[:, 4, :])
            ident = c_("ident")
            mm.wait_emptied(pe, len(mm.users) - 1)
            tp.wait_emptied(pe, len(tp.users) - 1)
            prime(pe, gate_filled, up_filled, at_filled, down_filled)
            with pe.Fori(0, rounds * PAIRS) as it:
                for par in range(2):
                    pe.wait_ge(xg_in[par], it * 16 + 16)
                    before = it + 1 if par == 0 else it + 2
                    pe.wait_ge(xt_act[1 - par], before)
                    pe.wait_ge(xt_dve[1 - par], before)
                    for k in range(KD):
                        ins = nc.tensor.transpose(XTB[k // 4][:, (k % 4) * P:(k % 4 + 1) * P],
                                                  xg[:, par, k * P:(k + 1) * P], ident)
                        if k % 4 == 3:
                            ins.then_inc((xt0_filled, xt1_filled)[k // 4][par], 1)

                def hidden(par, bank, n, loaded, filled):
                    w = ring6[3 * par + n].rearrange("p (k n) -> p k n", k=KD)
                    pe.wait_ge(loaded[par], it * 16 + 16)
                    for k in range(KD):
                        ins = nc.tensor.matmul(bank, xgT[:, par, k, :], w[:, k, :], start=(k == 0), stop=(k == KD - 1))
                    ins.then_inc(filled[par], 1)

                def gate(par):
                    pe.wait_ge(xt_act[par], it + 2)
                    pe.wait_ge(xt_dve[par], it + 2)
                    pe.wait_ge(sg_done[1 - par], it + 1 if par == 0 else it + 2)
                    hidden(par, GATE, 0, gate_in, gate_filled)

                def up(par):
                    pe.wait_ge(ac_done[par], it + 1)
                    hidden(par, UP[par], 1, up_in, up_filled)

                def turn(par):
                    pe.wait_ge(ac_done[par], it + 2)
                    pe.wait_ge(at_done[1 - par], it + 1 if par == 0 else it + 2)
                    for k in range(4):
                        ins = nc.tensor.transpose(AT[:, k * P:(k + 1) * P], ac[:, par, k * P:(k + 1) * P], ident)
                    ins.then_inc(at_filled[par], 1)

                def down(par):
                    w = ring6[3 * par + 2].rearrange("p (k n) -> p k n", k=4)
                    pe.wait_ge(down_in[par], it * 16 + 16)
                    pe.wait_ge(at_done[par], it + 2)
                    for c in range(2):
                        pe.wait_ge((y_act, y_dve)[c][1 - par], it + 1 if par == 0 else it + 2)
                        for k in range(4):
                            ins = nc.tensor.matmul(Y[c], acT[:, par, k, :], w[:, k, c * CH:(c + 1) * CH],
                                                   start=(k == 0), stop=(k == 3))
                        ins.then_inc((y0_filled, down_filled)[c][par], 1)

                gate(0)
                up(0)
                gate(1)
                turn(0)
                up(1)
                down(0)
                turn(1)
                down(1)

        @block.scalar
        def _(act):
            steps = [0]

            def own(ins):
                steps[0] += 1
                ins.then_inc(act_step, 1)
                act.wait_ge(act_step, steps[0])

            def empty(ring, m, dst, n, func, scale=1.0, cols=CH, src=None):
                ring.wait_filled(act, m)
                nc.scalar.activation(dst, ring.bank(m)[0:n, 0:cols] if src is None else src, func,
                                     scale=scale).then_inc(ring.done(m), 1)

            def turn_in(first, u, n, dst):
                m = first + u
                empty(tp, m, dst, P, ACT.Copy, src=tp.bank(m)[:, 0:4 * n].rearrange("p (k n) -> p k n", k=4))

            key_copy = copy_keys(tp, KT, kt_read)

            act.wait_ge(c_in, 32)
            nc.scalar.activation(crow[0:9, :], crow[0:9, :], ACT.Silu).then_inc(silu_done, 1)
            act.wait_ge(x_in, 32)
            act.wait_ge(stat_set, 1)
            for i in range(TILES):
                n = ROWS[i]
                if i:
                    act.wait_ge(sq_done, i)
                nc.scalar.activation(junk[0:n, :], x0[0:n, i, :], ACT.Square,
                                     accum_out=ss[0:n, i:i + 1]).then_inc(sq_done, 1)
            act.wait_ge(var_done, 1)
            nc.scalar.activation(rs, rs, ACT.Sqrt).then_inc(sqrt_done, 1)
            for i in range(TILES):
                for half in range(2):
                    turn_in(tp.first["h"], 2 * i + half, ROWS[i],
                            hT[:, 4 * half:4 * half + 4, i * P:i * P + ROWS[i]])
            for j in range(2):
                for i in range(TILES):
                    n = ROWS[i]
                    empty(mm, mm.first["v"] + TILES * j + i, mix[0:n, i, j * CH:(j + 1) * CH], n, ACT.Gelu_apprx_tanh)
            act.wait_ge(lnvar, 1)
            nc.scalar.activation(lnr, lnr, ACT.Sqrt).then_inc(lnsqrt, 1)
            for j in range(2):
                for i in range(TILES):
                    n = ROWS[i]
                    empty(mm, mm.first["u"] + TILES * j + i, x0[0:n, i, j * CH:(j + 1) * CH], n, ACT.Gelu_apprx_tanh)
            for i in range(TILES):
                for half in range(2):
                    turn_in(tp.first["ob"], 2 * i + half, ROWS[i],
                            obT[:, 4 * half:4 * half + 4, i * P:i * P + ROWS[i]])
            act.wait_ge(vout, 16)
            for j in range(2):
                for i in range(TILES):
                    n = ROWS[i]
                    empty(mm, mm.first["gb"] + TILES * j + i, mix[0:n, i, j * CH:(j + 1) * CH], n, ACT.Sigmoid)
            for g in range(3):
                for i in range(TILES):
                    n = ROWS[i]
                    empty(mm, mm.first[f"q{g}"] + i, qn[0:n, i, :], n, ACT.Copy, scale=DH ** -0.5)
                if g:
                    act.wait_ge(kv_out, 16 * KV_OUTS[g - 1])
                for i in range(TILES):
                    n = ROWS[i]
                    m = mm.first[f"w{g}"] + i
                    mm.wait_filled(act, m)
                    ins = nc.scalar.activation(vn[:, i, :] if i < 4 else vs[0:NS, g, :], mm.bank(m)[0:n, :], ACT.Copy)
                    ins.then_inc(mm.done(m), 1)
                for j, (dst, keep) in enumerate(((qT, qTs), (kT, kTs))):
                    for i in range(TILES):
                        turn_in(tp.first[f"qk{g}"], TILES * j + i, ROWS[i],
                                dst[:, :, i * P:(i + 1) * P] if i < 4 else keep[:, g, :, :])
                for _, i, keys in GT[4 * g:4 * g + 4]:
                    nk = len(keys)
                    act.wait_ge(scored, 4 * g + i + 1)
                    for hp in range(H):
                        ins = nc.scalar.activation(sc[:, hp, 0:nk * P], sc[:, hp, 0:nk * P], ACT.Exp,
                                                   bias=oe[:, i % 2, AW + hp:AW + hp + 1],
                                                   accum_out=oe[:, i % 2, AW + H + hp:AW + H + hp + 1])
                    ins.then_inc(exped, 1)
                    for kk in range(nk):
                        for par in range(2):
                            turn_in(tp.first[f"p{g}{i}"], 2 * kk + par, P, pT[:, kk, 4 * par:4 * par + 4, :])
            for i in range(4):
                act.wait_ge(lse_dif, i + 1)
                nc.scalar.activation(fw, fw, ACT.Exp, scale=-1.0).then_inc(lse_exp, 1)
                turn_in(tp.first["o"], i, P, oT[:, :, i * P:(i + 1) * P])
            for b in range(NB + 2):
                if b < NB:
                    for x in range(0, XT, 2):
                        key_copy(act, nc.scalar, b, x)
                if b >= 2:
                    u = tp.first[f"ot{b - 2}"]
                    tp.wait_filled(act, u)
                    nc.scalar.activation(oT[:, :, SEQ + (b - 2) * NT:SEQ + (b - 1) * NT],
                                         tp.bank(u)[:, 0:4 * NT].rearrange("p (j n) -> p j n", j=4),
                                         ACT.Copy).then_inc(tp_act, 1)
                if b < NB:
                    act.wait_ge(s_max, b + 1)
                    for g in range(3):
                        nc.scalar.activation(ssc[0:NS, b % 2, g, :], ssc[0:NS, b % 2, g, :], ACT.Exp,
                                             bias=snm[0:NS, b % 2, g:g + 1],
                                             accum_out=sden[0:NS, b % 2, g:g + 1])
                    nc.scalar.activation(sf[0:NS, b % 2, :], sf[0:NS, b % 2, :], ACT.Exp, scale=-1.0).then_inc(s_exp, 1)
            for j in range(2):
                for i in range(TILES):
                    n = ROWS[i]
                    empty(mm, mm.first["ga"] + TILES * j + i, sga[0:n, i, j * CH:(j + 1) * CH], n, ACT.Sigmoid)
            for i in range(TILES):
                for half in range(2):
                    turn_in(tp.first["mix"], 2 * i + half, ROWS[i],
                            mixT[:, 4 * half:4 * half + 4, i * P:i * P + ROWS[i]])
            mm.wait_filled(act, mm.first["wo"] + 9)
            for i in range(TILES):
                n = ROWS[i]
                act.wait_ge(x1_done, i + 1)
                if i:
                    act.wait_ge(sq2, i)
                nc.scalar.activation(junk[0:n, :], x1[0:n, i, :], ACT.Square,
                                     accum_out=ss[0:n, i:i + 1]).then_inc(sq2, 1)
            act.wait_ge(var2, 1)
            nc.scalar.activation(rs, rs, ACT.Sqrt).then_inc(sqrt2, 1)
            for i in range(TILES):
                for half in range(2):
                    turn_in(tp.first["h2"], 2 * i + half, ROWS[i],
                            h2T[:, 4 * half:4 * half + 4, i * P:i * P + ROWS[i]])
            act.wait_ge(rt_exp_in, 1)
            nc.scalar.activation(eg, eg, ACT.Exp).then_inc(rt_exp, 1)
            act.wait_ge(rt_exp_in, 2)
            nc.scalar.activation(w2, w2, ACT.Exp).then_inc(rt_exp, 1)
            rounds = rounds_of(act)
            prime(act, xt_act, sg_done, at_done, y_act)
            with act.Fori(0, rounds * PAIRS) as it:
                for par in range(2):
                    act.wait_ge(xt0_filled[par], it + 1)
                    act.wait_ge(up_filled[par], it + 1)
                    nc.scalar.activation(xgT[:, par, 0:4, :], psum[:, 0, :].rearrange("p (k n) -> p k n", k=4),
                                         ACT.Copy).then_inc(xt_act[par], 1)
                for par in range(2):
                    act.wait_ge(gate_filled[par], it + 2)
                    act.wait_ge(ac_done[par], it + 1)
                    nc.scalar.activation(sg[:, par, :], psum[:, 2, :], ACT.Silu).then_inc(sg_done[par], 1)
                for par in range(2):
                    act.wait_ge(at_filled[par], it + 2)
                    act.wait_ge(down_filled[par], it + 1)
                    nc.scalar.activation(acT[:, par, :, :], psum[:, 5, :].rearrange("p (k n) -> p k n", k=4),
                                         ACT.Copy).then_inc(at_done[par], 1)
                    act.wait_ge(y0_filled[par], it + 1)
                    act.wait_ge(y_out[par], it * 16 + 16)
                    nc.scalar.activation(yb[:, par, 0:CH], psum[:, 6, :], ACT.Copy).then_inc(y_act[par], 1)
            for i in range(TILES):
                n = ROWS[i]
                act.wait_ge(x2_done, i + 1)
                if i:
                    act.wait_ge(sq3, i)
                nc.scalar.activation(gain[0:n, :], x1[0:n, i, :], ACT.Square,
                                     accum_out=ss[0:n, i:i + 1]).then_inc(sq3, 1)
                act.wait_ge(var3, i + 1)
                nc.scalar.activation(rs[0:n, i:i + 1], rs[0:n, i:i + 1], ACT.Sqrt).then_inc(sqrt3, 1)

        @block.vector
        def _(dve):
            steps = [0]

            def own(ins):
                steps[0] += 1
                ins.then_inc(dve_step, 1)
                dve.wait_ge(dve_step, steps[0])

            V = nc.vector
            V.memset(stat[:, 152:256], 1.0).then_inc(stat_set, 1)
            dve.wait_ge(stat_set, 1)
            m = tp.first["c"]
            dve.wait_ge(const_in, 16)
            tp.wait_filled(dve, m)
            V.tensor_copy(cT.rearrange("p k n -> p (k n)"), tp.bank(m)[:, 0:KD * 9]).then_inc(tp_dve, 1)

            dve.wait_ge(gain_in, 16)
            for n in range(4):
                m = mm.first["ada1"] + 3 * n
                dve.wait_ge(bias_in[n % 2], 16 * (n // 2 + 1))
                mm.wait_filled(dve, m)
                V.tensor_tensor(modrow[0:9, n % 2, :], mm.bank(m)[0:9, :], modbias[0:9, n % 2, :],
                                ALU.add).then_inc(mm_dve, 1)
                for s in range(2):
                    w = (P, NS)[s]
                    m += 1
                    mm.wait_filled(dve, m)
                    dst, col = mod[0:w, n // 2, s, (n % 2) * CH:(n % 2 + 1) * CH], slice((n % 2) * CH, (n % 2 + 1) * CH)
                    if n // 2 == 1:
                        ins = V.scalar_tensor_tensor(out=dst, in0=mm.bank(m)[0:w, :], scalar=1.0, in1=gain[0:w, col],
                                                     op0=ALU.add, op1=ALU.mult)
                    else:
                        ins = V.tensor_copy(dst, mm.bank(m)[0:w, :])
                    ins.then_inc(mm_dve, 1)
            dve.wait_ge(sq_done, TILES)
            V.tensor_scalar(rs, ss, 1.0 / D, EPS, ALU.mult, ALU.add).then_inc(var_done, 1)
            dve.wait_ge(sqrt_done, 1)
            own(V.reciprocal(rs, rs))
            dve.wait_ge(mm_dve, 12)
            for i in range(TILES):
                n, s = ROWS[i], i // 4
                own(V.scalar_tensor_tensor(out=x0[0:n, i, :], in0=x0[0:n, i, :], scalar=rs[0:n, i:i + 1],
                                           in1=mod[0:n, 1, s, :], op0=ALU.mult, op1=ALU.mult))
                V.tensor_tensor(x0[0:n, i, :], x0[0:n, i, :], mod[0:n, 0, s, :], ALU.add).then_inc(hn_done, 1)
            for half in range(2):
                m = tp.first["sgu"] + half
                tp.wait_filled(dve, m)
                V.tensor_tensor(sguT[:, 4 * half:4 * half + 4, :], tp.bank(m)[:, :].rearrange("p (g n) -> p g n", g=4),
                                c_("tril").unsqueeze(1).to_broadcast([P, 4, P]), ALU.mult).then_inc(tp_dve, 1)
            m = tp.first["sgu"] + 2
            tp.wait_filled(dve, m)
            V.tensor_copy(sgubT, tp.bank(m)[:, 0:H]).then_inc(tp_dve, 1)
            for i in range(TILES):
                n = ROWS[i]
                mm.wait_emptied(dve, mm.first["v"] + TILES + i)
                for half in range(2):
                    ins = V.bn_stats(bns[0:n, i, 6 * half:6 * half + 6], mix[0:n, i, half * CH:(half + 1) * CH])
                own(ins)
                own(V.bn_aggr(mv[0:n, i, :], bns[0:n, i, :]))
                ins = V.tensor_scalar(lnr[0:n, i:i + 1], mv[0:n, i, 1:2], EPS, None, ALU.add)
            ins.then_inc(lnvar, 1)
            m = tp.first["rep"]
            tp.wait_filled(dve, m)
            V.tensor_copy(sgubTs[0:NS, :], tp.bank(m)[0:NS, NS:NS + H]).then_inc(dve_step, 1)
            steps[0] += 1
            V.tensor_tensor(sguTs[0:NS].rearrange("p g (b t) -> p g b t", b=NB),
                            tp.bank(m)[0:NS, 0:NS].rearrange("p (g t) -> p g t", g=H).unsqueeze(2).to_broadcast([NS, H, NB, NT]),
                            c_("blkt", NS).rearrange("p (b t) -> p b t", b=NB).unsqueeze(1).to_broadcast([NS, H, NB, NT]),
                            ALU.mult).then_inc(tp_dve, 1)
            dve.wait_ge(lnsqrt, 1)
            own(V.reciprocal(lnr, lnr))
            dve.wait_ge(ln_in, 32)
            for i in range(TILES):
                n = ROWS[i]
                v = mix[0:n, i, :]
                own(V.tensor_scalar(v, v, mv[0:n, i, 0:1], lnr[0:n, i:i + 1], ALU.subtract, ALU.mult))
                own(V.tensor_tensor(v, v, lng[0:n, :], ALU.mult))
                V.tensor_tensor(v, v, lnb[0:n, :], ALU.add).then_inc(vn_done, 1)
            for i in range(TILES):
                n = ROWS[i]
                for half in range(2):
                    m = mm.first["sgu"] + 2 * i + half
                    mm.wait_filled(dve, m)
                    for k in range(4):
                        g = 4 * half + k
                        u = x0[0:n, i, g * P:(g + 1) * P]
                        b = (sgubT if i < 4 else sgubTs)[0:n, g:g + 1]
                        ins = V.scalar_tensor_tensor(out=u, in0=mm.bank(m)[0:n, k * P:(k + 1) * P], scalar=b, in1=u,
                                                     op0=ALU.add, op1=ALU.mult)
                    ins.then_inc(mm_dve, 1)
            for j in range(2):
                for i in range(TILES):
                    n = ROWS[i]
                    m = mm.first["pb"] + TILES * j + i
                    x = mix[0:n, i, j * CH:(j + 1) * CH]
                    mm.wait_filled(dve, m)
                    mm.wait_emptied(dve, mm.first["gb"] + TILES * j + i)
                    V.tensor_tensor(x, mm.bank(m)[0:n, :], x, ALU.mult).then_inc(mm_dve, 1)
            for g in range(3):
                if g:
                    dve.wait_ge(kv_out, 16 * KV_OUTS[g - 1])
                for i in range(TILES):
                    n = ROWS[i]
                    m = mm.first[f"k{g}"] + i
                    mm.wait_filled(dve, m)
                    ins = V.tensor_copy(kn[0:n, i, :], mm.bank(m)[0:n, :])
                    ins.then_inc(mm_dve, 1)
                dve.wait_ge(abias_in, 16 * (g + 2))
                for _, i, keys in GT[4 * g:4 * g + 4]:
                    nk, job = len(keys), 4 * g + i
                    for kk in range(nk):
                        for par in range(2):
                            m = mm.first[f"s{g}{i}"] + 2 * kk + par
                            mm.wait_filled(dve, m)
                            kind = 0 if g == 0 and nk == 2 and kk == 0 else 1
                            ins = V.tensor_tensor(sc[:, 4 * par:4 * par + 4, kk * P:(kk + 1) * P],
                                                  mm.bank(m)[:, :].rearrange("p (j n) -> p j n", j=4),
                                                  abias[:, kind, 4 * par:4 * par + 4, :], ALU.add)
                            ins.then_inc(mm_dve, 1)
                    if job >= 2:
                        dve.wait_ge(o_out[i % 2], 16 * (job // 2))
                    mm.wait_emptied(dve, mm.first[f"s{g}{i}"] + 2 * nk - 1)
                    V.tensor_reduce(oe[:, i % 2, AW:AW + H], sc[:, :, 0:nk * P], AX.X, ALU.max,
                                    negate=True).then_inc(scored, 1)
                    m = mm.first[f"o{g}{i}"]
                    mm.wait_filled(dve, m)
                    V.tensor_copy(oe[:, i % 2, 0:AW], mm.bank(m)[:, :]).then_inc(mm_dve, 1)
            dve.wait_ge(oin_in, 48)
            for i in range(4):
                r = oin[:, i, :].rearrange("p (g n) -> p g n", g=3)
                nm, den = r[:, :, AW:AW + H], r[:, :, AW + H:AW + 2 * H]
                own(V.tensor_reduce(nmin, nm.rearrange("p g h -> p h g"), AX.X, ALU.min))
                V.tensor_tensor(fw, nm, nmin.unsqueeze(1).to_broadcast([P, 3, H]), ALU.subtract).then_inc(lse_dif, 1)
                dve.wait_ge(lse_exp, i + 1)
                own(V.tensor_tensor(fd, fw, den, ALU.mult))
                own(V.tensor_reduce(nmin, fd.rearrange("p g h -> p h g"), AX.X, ALU.add))
                own(V.reciprocal(nmin, nmin))
                own(V.tensor_tensor(fw, fw, nmin.unsqueeze(1).to_broadcast([P, 3, H]), ALU.mult))
                if i >= 2:
                    dve.wait_ge(tp_filled, tp.first["o"] + i - 1)
                for g in range(3):
                    w = fw[:, g, :].rearrange("p (par j) -> p j par", par=2).unsqueeze(3).to_broadcast([P, 4, 2, DH])
                    o = r[:, g, 0:AW].rearrange("p (j par d) -> p j par d", j=4, par=2)
                    own(V.tensor_tensor(o, o, w, ALU.mult))
                own(V.tensor_tensor(oc[:, i % 2, :], r[:, 0, 0:AW], r[:, 1, 0:AW], ALU.add))
                V.tensor_tensor(oc[:, i % 2, :], oc[:, i % 2, :], r[:, 2, 0:AW], ALU.add).then_inc(oc_done, 1)
            def spread_q(b):
                if b >= 2:
                    mm.wait_filled(dve, mm.first[f"ss{b - 2}"] + 2)
                for half in range(2):
                    r = slice(64 * half, 64 * half + 64)
                    blocks = Qm[r, b % 2, :]

                    def spread(block, count):
                        a = block * 256 + half
                        return blocks[:, a:a + 66 * count].rearrange("p (n x) -> p n x", x=66)

                    for g, block in ((0, 0), (1, 13), (2, 14)):
                        V.tensor_copy(spread(block, 4)[:, :, 0:64].rearrange("p j (t y) -> p j t y", y=8)[:, :, :, 0],
                                      qTs[r, g, :, b * NT:(b + 1) * NT])
                    V.tensor_copy(spread(1, 16)[:, :, 0:64].rearrange("p (r j) (u y) -> p r j u y", j=4, y=32)[:, :, :, :, 0],
                                  qTs[r, 1, :, b * NT:(b + 1) * NT].rearrange("p j (u r) -> p r j u", r=4))
                    ins = V.tensor_copy(spread(5, 32)[:, :, 0].rearrange("p (t j) -> p t j", j=4),
                                        qTs[r, 2, :, b * NT:(b + 1) * NT].rearrange("p j t -> p t j"))
                ins.then_inc(q_spread, 1)

            key_copy = copy_keys(tp, KT, kt_read)
            own(V.memset(pTm, 0.0))
            tp.wait_emptied(dve, tp.first["qk2"] + 2 * TILES - 1)
            own(V.memset(Qm, 0.0))
            spread_q(0)
            for b in range(NB + 1):
                if b < NB:
                    for x in range(1, XT, 2):
                        key_copy(dve, V, b, x)
                    dve.wait_ge(sb_in[b % 2], 16 * (b // 2 + 1))
                    for g in range(3):
                        m = mm.first[f"ss{b}"] + g
                        mm.wait_filled(dve, m)
                        if b >= 2 and g == 0:
                            tp.wait_filled(dve, tp.first[f"pt{b - 2}"])
                        V.tensor_tensor(ssc[0:NS, b % 2, g, :], mm.bank(m)[0:NS, 0:KEYS], sbias[0:NS, b % 2, g, :],
                                        ALU.add).then_inc(mm_dve, 1)
                    mm.wait_emptied(dve, mm.first[f"ss{b}"] + 2)
                    nm = snm[0:NS, b % 2, :]
                    own(V.tensor_reduce(nm, ssc[0:NS, b % 2, :, :], AX.X, ALU.max, negate=True))
                    own(V.tensor_reduce(smin[0:NS, 0:1], nm, AX.X, ALU.min))
                    V.tensor_scalar(sf[0:NS, b % 2, :], nm, smin[0:NS, 0:1], None, ALU.subtract).then_inc(s_max, 1)
                    if b + 1 < NB:
                        spread_q(b + 1)
                if b >= 1:
                    c, f = b - 1, sf[0:NS, (b - 1) % 2, :]
                    u = tp.first[f"pt{c}"]
                    tp.wait_filled(dve, u)
                    if c:
                        mm.wait_filled(dve, mm.first[f"so{c - 1}"])
                    bank = tp.bank(u)
                    V.tensor_copy(pTn[0:NS, :, :], bank[0:NS, 3 * NS:6 * NS].rearrange("p (g n) -> p g n", g=3))
                    V.tensor_copy(pTm[:, 0:NS], bank[:, 0:NS])
                    for v in range(2):
                        V.tensor_copy(pTm[:, NS + 32 * v:NS + 32 * v + 288].rearrange("p (r x) -> p r x", x=72)[:, :, 0:H],
                                      bank[:, NS + 32 * v:NS + 32 * v + 32].rearrange("p (r h) -> p r h", h=H))
                    V.tensor_copy(pTm[:, 5 * NS:5 * NS + 576].rearrange("p (t x) -> p t x", x=72)[:, :, 0:H],
                                  bank[:, 2 * NS:3 * NS].rearrange("p (t h) -> p t h", h=H)).then_inc(tp_dve, 1)
                    m = mm.first[f"so{c}"]
                    mm.wait_filled(dve, m)
                    if c:
                        tp.wait_filled(dve, tp.first[f"ot{c - 1}"])
                    V.tensor_tensor(om[0:NS, :], mm.bank(m)[0:NS, :], c_("dmask", NS), ALU.mult).then_inc(mm_dve, 1)
                if b < NB:
                    f, d = sf[0:NS, b % 2, :], sden[0:NS, b % 2, :]
                    dve.wait_ge(s_exp, b + 1)
                    own(V.tensor_tensor(d, d, f, ALU.mult))
                    own(V.tensor_reduce(smin[0:NS, 1:2], d, AX.X, ALU.add))
                    own(V.reciprocal(smin[0:NS, 1:2], smin[0:NS, 1:2]))
                    own(V.tensor_scalar(f, f, smin[0:NS, 1:2], None, ALU.mult))
                    V.tensor_tensor(ssc[0:NS, b % 2, :, :], ssc[0:NS, b % 2, :, :],
                                    f.unsqueeze(2).to_broadcast([NS, 3, KEYS]), ALU.mult).then_inc(p_ready, 1)
            for c in range(2):
                for i in range(TILES):
                    n = ROWS[i]
                    m = mm.first["pa"] + TILES * c + i
                    s_, x = sga[0:n, i, c * CH:(c + 1) * CH], mix[0:n, i, c * CH:(c + 1) * CH]
                    mm.wait_filled(dve, m)
                    mm.wait_emptied(dve, mm.first["ga"] + TILES * c + i)
                    own(V.tensor_tensor(s_, mm.bank(m)[0:n, :], s_, ALU.mult))
                    V.tensor_tensor(x, x, s_, ALU.add).then_inc(mm_dve, 1)

            def modulate(name, rows, biases, base, gain_n, targets):
                dve.wait_ge(gain_in, 16 * gain_n)
                for n in range(6):
                    m = mm.first[name] + 3 * n
                    dve.wait_ge(bias_in[n % 2], 16 * (base + n // 2 + 1))
                    mm.wait_filled(dve, m)
                    V.tensor_tensor(rows[0:9, n % 2, :], mm.bank(m)[0:9, :], biases[0:9, n % 2, :], ALU.add).then_inc(mm_dve, 1)
                    for s in range(2):
                        w = (P, NS)[s]
                        m += 1
                        mm.wait_filled(dve, m)
                        col = slice((n % 2) * CH, (n % 2 + 1) * CH)
                        which = targets[n // 2]
                        dst = mod[0:w, which, s, col]
                        if which == 1:
                            ins = V.scalar_tensor_tensor(out=dst, in0=mm.bank(m)[0:w, :], scalar=1.0, in1=gain[0:w, col],
                                                         op0=ALU.add, op1=ALU.mult)
                        else:
                            ins = V.tensor_copy(dst, mm.bank(m)[0:w, :])
                        ins.then_inc(mm_dve, 1)

            modulate("ada2", modrow2, modbias2, 2, 2, (2, 0, 1))
            dve.wait_ge(x1_in, 32)
            mm.wait_emptied(dve, mm.first["ada2"] + 17)
            for j in range(2):
                for i in range(TILES):
                    n, s = ROWS[i], i // 4
                    m = mm.first["wo"] + TILES * j + i
                    x = x1[0:n, i, j * CH:(j + 1) * CH]
                    mm.wait_filled(dve, m)
                    if j and i:
                        dve.wait_ge(x1_done, i)
                    V.tensor_tensor(gt_tmp[0:n, :], mm.bank(m)[0:n, :], mod[0:n, 2, s, j * CH:(j + 1) * CH],
                                    ALU.mult).then_inc(mm_dve, 1)
                    mm.wait_emptied(dve, m)
                    ins = V.tensor_tensor(x, x, gt_tmp[0:n, :], ALU.add)
                    if j:
                        ins.then_inc(x1_done, 1)
                    else:
                        own(ins)
            dve.wait_ge(sq2, TILES)
            V.tensor_scalar(rs, ss, 1.0 / D, EPS, ALU.mult, ALU.add).then_inc(var2, 1)
            dve.wait_ge(sqrt2, 1)
            own(V.reciprocal(rs, rs))
            for i in range(TILES):
                n, s = ROWS[i], i // 4
                if i >= 2:
                    dve.wait_ge(h2_out[i % 2], 16 * (i // 2))
                    tp.wait_filled(dve, tp.first["h2"] + 2 * (i - 2) + 1)
                own(V.scalar_tensor_tensor(out=hrow[0:n, i % 2, :], in0=x1[0:n, i, :], scalar=rs[0:n, i:i + 1],
                                           in1=mod[0:n, 1, s, :], op0=ALU.mult, op1=ALU.mult))
                V.tensor_tensor(hrow[0:n, i % 2, :], hrow[0:n, i % 2, :], mod[0:n, 0, s, :], ALU.add).then_inc(h2_done, 1)
            own(V.memset(rt(0, 780), 0.0))
            dve.wait_ge(rt_in, 16 * 7)
            for i in range(TILES):
                n = ROWS[i]
                m = mm.first["rt"] + i
                mm.wait_filled(dve, m)
                V.tensor_tensor(lg[0:n, i, :], mm.bank(m)[0:n, 0:20], brt[0:n, :], ALU.add).then_inc(mm_dve, 1)
            mm.wait_emptied(dve, mm.first["rt"] + TILES - 1)
            iota4 = c_("iota")[:, 0:4].unsqueeze(1).to_broadcast([P, TILES, 4])

            def wide(a):
                return a.unsqueeze(2).to_broadcast([P, TILES, 4])

            def first_best(values, best, onehot):
                own(V.tensor_reduce(best, values, AX.X, ALU.max))
                own(V.tensor_tensor(eq4, values, wide(best), ALU.is_equal))
                own(V.scalar_tensor_tensor(out=cand4, in0=eq4, scalar=-99.0, in1=iota4, op0=ALU.mult, op1=ALU.add))
                own(V.tensor_reduce(id5, cand4, AX.X, ALU.min))
                own(V.tensor_scalar(id5, id5, 99.0, None, ALU.add))
                own(V.tensor_tensor(onehot, iota4, wide(id5), ALU.is_equal))

            first_best(lg[:, :, 0:4], sc5, on_g)
            V.tensor_tensor(eg, lg[:, :, 0:4], wide(sc5), ALU.subtract).then_inc(rt_exp_in, 1)
            own(V.tensor_tensor(tmp5, lg[:, :, 4:20].rearrange("p i (g e) -> p i g e", g=4),
                                on_g.unsqueeze(3).to_broadcast([P, TILES, 4, 4]), ALU.mult))
            own(V.tensor_reduce(esel, tmp5.rearrange("p i g e -> p i e g"), AX.X, ALU.add))
            first_best(esel, e1m, on_1)
            own(V.scalar_tensor_tensor(out=esel2, in0=on_1, scalar=NEG, in1=esel, op0=ALU.mult, op1=ALU.add))
            first_best(esel2, e2m, on_2)
            dve.wait_ge(rt_exp, 1)
            own(V.tensor_reduce(gp, eg, AX.X, ALU.add))
            own(V.reciprocal(gp, gp))
            V.tensor_tensor(w2, e2m, e1m, ALU.subtract).then_inc(rt_exp_in, 1)
            for on, mk in ((on_1, m1), (on_2, m2)):
                own(V.tensor_tensor(mk.rearrange("p i (g e) -> p i g e", g=4),
                                    on_g.unsqueeze(3).to_broadcast([P, TILES, 4, 4]),
                                    on.unsqueeze(2).to_broadcast([P, TILES, 4, 4]), ALU.mult))
            own(V.tensor_tensor(mask, m1, m2, ALU.add))
            V.tensor_tensor(mask, mask, c_("valid").unsqueeze(2).to_broadcast([P, TILES, 16]), ALU.mult).then_inc(mask_done, 1)
            dve.wait_ge(rt_exp, 2)
            own(V.tensor_scalar(w1, w2, 1.0, None, ALU.add))
            own(V.reciprocal(w1, w1))
            own(V.tensor_tensor(w1, w1, gp, ALU.mult))
            own(V.tensor_tensor(w2, w2, w1, ALU.mult))
            modulate("ada3", modrow2, modbias2, 5, 3, (2, 0, 1))
            m = tp.first["pos"]
            tp.wait_filled(dve, m)
            own(V.tensor_tensor(place, tp.bank(m)[:, 0:80].rearrange("p (i e) -> p i e", e=16),
                                c_("ebase").unsqueeze(1).to_broadcast([P, TILES, 16]), ALU.add))
            own(V.tensor_reduce(rounds_f, tp.bank(m)[:, 80:96], AX.X, ALU.max))
            own(V.tensor_scalar(sc5, c_("iota")[:, 0:TILES], float(CAP), rounds_f, ALU.mult, ALU.is_lt))
            own(V.tensor_reduce(rounds_f, sc5, AX.X, ALU.add))
            own(V.tensor_scalar(rounds_f, rounds_f, 1.0, None, ALU.max))
            V.tensor_copy(rounds_u, rounds_f).then_inc(tp_dve, 1)
            for k, mk in enumerate((m1, m2)):
                own(V.tensor_tensor(pick, place, mk, ALU.mult))
                own(V.tensor_reduce(rowf[:, k, :], pick, AX.X, ALU.add))
            V.tensor_copy(row_u, rowf).then_inc(rows_done, 1)
            rounds = rounds_of(dve)
            prime(dve, xt_dve, ac_done, y_dve)
            with dve.Fori(0, rounds * PAIRS) as it:
                for par in range(2):
                    dve.wait_ge(xt1_filled[par], it + 1)
                    dve.wait_ge(up_filled[par], it + 1)
                    V.tensor_copy(xgT[:, par, 4:8, :], psum[:, 1, :].rearrange("p (k n) -> p k n", k=4)).then_inc(xt_dve[par], 1)
                for par in range(2):
                    dve.wait_ge(up_filled[par], it + 2)
                    dve.wait_ge(sg_done[par], it + 2)
                    dve.wait_ge(at_filled[par], it + 1)
                    V.tensor_tensor(ac[:, par, :], psum[:, 3 + par, :], sg[:, par, :], ALU.mult).then_inc(ac_done[par], 1)
                for par in range(2):
                    dve.wait_ge(down_filled[par], it + 2)
                    dve.wait_ge(y_out[par], it * 16 + 16)
                    V.tensor_copy(yb[:, par, CH:D], psum[:, 7, :]).then_inc(y_dve[par], 1)
            for i in range(TILES):
                n, s = ROWS[i], i // 4
                y1, y2 = yg[0:n, i % 2, 0, :], yg[0:n, i % 2, 1, :]
                x = x1[0:n, i, :]
                dve.wait_ge(yg_in2[i % 2], 16 * (i // 2 + 1))
                own(V.tensor_scalar(y1, y1, w1[0:n, i:i + 1], None, ALU.mult))
                own(V.scalar_tensor_tensor(out=y1, in0=y2, scalar=w2[0:n, i:i + 1], in1=y1, op0=ALU.mult, op1=ALU.add))
                own(V.tensor_tensor(y1, y1, mod[0:n, 2, s, :], ALU.mult))
                V.tensor_tensor(x, x, y1, ALU.add).then_inc(x2_done, 1)
                dve.wait_ge(sq3, i + 1)
                V.tensor_scalar(rs[0:n, i:i + 1], ss[0:n, i:i + 1], 1.0 / D, EPS, ALU.mult, ALU.add).then_inc(var3, 1)
                dve.wait_ge(sqrt3, i + 1)
                own(V.reciprocal(rs[0:n, i:i + 1], rs[0:n, i:i + 1]))
                own(V.scalar_tensor_tensor(out=x, in0=x, scalar=rs[0:n, i:i + 1], in1=mod[0:n, 1, s, :],
                                           op0=ALU.mult, op1=ALU.mult))
                V.tensor_tensor(x, x, mod[0:n, 0, s, :], ALU.add).then_inc(y_done, 1)


_INS = ["x_prompt", "x_sample", "cache_kv_w128", "cache_kv_w512", "cache_kv_w2048", "c_prompt", "c_sample", "w_ada",
        "b_ada", "norm1_g", "norm2_g", "w_in", "sgu_ln_g", "sgu_ln_b", "sgu_w", "sgu_b", "w_pa", "w_pb", "w_o",
        "w_route_group", "b_route_group", "w_route_expert", "b_route_expert", "w_gate", "w_up", "w_down", "normf_g",
        "w_ada_final", "b_ada_final"]
_OUTS = [(1, SEQ, D), (NB, NT, D)] + [(1, 1, min(w, SEQ), 2, H, DH) for w in WINS] + [(1, NB, NT, 2, H, DH)] * 3 + [
    (1, NB, NT, D)]


def kernel(**inputs):
    import numpy as _np
    import concourse.bacc as _bacc
    from concourse import mybir as _mybir
    from concourse.bass_utils import run_bass_kernel_spmd as _run

    nc = _bacc.Bacc("TRN2", target_bir_lowering=False, num_devices=1)
    arrays, t = {}, {}
    given = {name: _np.ascontiguousarray(inputs[name]) for name in _INS}
    given |= {"consts": constants(), "pbias": prompt_bias(), "sbias": sample_bias(),
              "empty_slots": empty_slots(), "token_places": token_places()}
    for name, a in given.items():
        arrays[f"in_{name}_dram"] = a
        t[name] = nc.dram_tensor(f"in_{name}_dram", a.shape, _mybir.dt.from_np(a.dtype), kind="ExternalInput").ap()
    outs = [nc.dram_tensor(f"out_{i}_dram", s, _mybir.dt.float32, kind="ExternalOutput").ap() for i, s in enumerate(_OUTS)]
    named = {"y_prompt": outs[0][0], "y_sample": outs[1].rearrange("b t d -> (b t) d"),
             "kvp": [o[0, 0].rearrange("s c h d -> s (c h d)") for o in outs[2:5]],
             "kvs": [o[0].rearrange("b t c h d -> (b t) (c h d)") for o in outs[5:8]],
             "sgu_v": outs[8][0].rearrange("b t d -> (b t) d")}
    build(nc, t, named)
    r = _run(nc, [arrays], core_ids=[0])
    return tuple(r.results[0][f"out_{i}_dram"] for i in range(len(_OUTS)))
```

```python
from contextlib import ExitStack

import numpy as np

import concourse.bass as bass
from concourse import mybir

F32 = mybir.dt.float32
F32R = mybir.dt.float32r
U32 = mybir.dt.uint32
ALU = mybir.AluOpType
ACT = mybir.ActivationFunctionType
AX = mybir.AxisListType

P = 128
D = 1024
KD = D // P
SEQ, NB, NT = 512, 8, 8
NS = NB * NT
TILES = 5
ROWS = [P] * 4 + [NS]
TOK = SEQ + NS
H, DH = 8, 64
AW = H * DH
DILS = (1, 4, 16)
WINS = (128, 512, 2048)
STEPS = 128
CH = 512
E_ALL, FF = 16, 512
CAP = 128
EROWS = 640
EPS = 1e-6
NEG = -1e30
SLOTS = 4
SLOT = 4096
HALF = SLOT // 2
NC_CLS = (1, 4, 8)
CLS0 = (0, 1, 5)
XT = 13
KEYS = STEPS + NS
WORK = 14936
OW = AW + 16


def head_of(hp):
    return 2 * (hp % 4) + hp // 4


CST = {}


def const_layout():
    at = 0
    for name, width in (("ident", P), ("tril", P), ("before", P), ("ones", P), ("dmask", AW), ("seltok", NT),
                        ("selmod", P + NS), ("rep", NS), ("blk", NB), ("iota", 16), ("ebase", 16),
                        ("blkt", NS), ("valid", TILES)):
        CST[name] = (at, at + width)
        at += width
    return at


CONST_W = const_layout()


def slopes():
    n = 24
    return np.exp2(-8.0 * np.arange(1, n + 1, dtype=np.float32) / np.float32(n)).reshape(3, 8).astype(np.float32)


def constants():
    c = np.zeros((P, CONST_W), np.float32)

    def put(name, rows, a):
        c[:rows, CST[name][0]:CST[name][1]] = a

    i = np.arange(P)
    put("ident", P, np.eye(P))
    put("tril", P, i[:, None] <= i[None, :])
    put("before", P, i[:, None] < i[None, :])
    put("ones", P, 1.0)
    r = np.arange(NS)
    put("dmask", NS, (r % H)[:, None] == np.arange(AW)[None, :] // DH)
    put("seltok", NS, (r // H)[:, None] == np.arange(NT)[None, :])
    sel = np.zeros((2, 9, P + NS))
    sel[:, 0, :P] = 1
    sel[:, 1 + r // NT, P + r] = 1
    put("selmod", 18, sel.reshape(18, P + NS))
    put("rep", NT, np.arange(NT)[:, None] == (r % NT)[None, :])
    put("blk", NS, (r // NT)[:, None] == np.arange(NB)[None, :])
    put("blkt", NS, (r // NT)[:, None] == (r // NT)[None, :])
    put("iota", P, np.arange(16)[None, :])
    put("ebase", P, np.arange(16)[None, :] * EROWS)
    put("valid", P, (i[:, None] + P * np.arange(TILES)[None, :]) < TOK)
    return c


def empty_slots():
    row = np.arange(E_ALL * EROWS + CAP, dtype=np.uint32)
    return np.stack([0 * row, 2 * TOK + row % CAP], axis=1).astype(np.uint32)


def token_places():
    tok = np.arange(P)[:, None] + P * np.arange(TILES)[None, :]
    a = np.stack([np.stack([tok, 2 * tok + k], axis=-1) for k in range(2)], axis=1)
    return a.reshape(P, 4 * TILES).astype(np.uint32)


def prompt_bias():
    s = slopes()
    q, k = np.arange(P)[:, None], np.arange(P)[None, :]
    out = np.full((4, P, H, P), NEG, np.float32)
    for kind, g, dist, ok in ((0, 0, q + P - k, k >= q), (1, 0, q - k, k <= q), (2, 1, 4 * (q - k), k <= q),
                              (3, 2, 4 * (q - k), (k <= q) & ((q - k) % 4 == 0))):
        dist = dist.astype(np.float32)
        for hp in range(H):
            out[kind, :, hp][ok] = -(s[g, head_of(hp)] * dist)[ok]
    return out


def sample_bias():
    s = slopes()
    out = np.full((NB, NS, 3, KEYS), NEG, np.float32)
    for g, dil in enumerate(DILS):
        for t in range(NT):
            for h in range(H):
                row = t * H + h
                c = np.arange(STEPS)
                j = (t + WINS[g] - (c * dil + t % dil)) // dil
                ok = (j >= 0) & (j <= STEPS)
                out[:, row, g, :STEPS][:, ok] = -(s[g, h] * (dil * j).astype(np.float32))[ok]
                for n in range(t + 1):
                    if (t - n) % dil == 0:
                        for b in range(NB):
                            out[b, row, g, STEPS + b * NT + n] = -(s[g, h] * np.float32(t - n))
    return out


def copy_keys(tp, KT, kt_read):
    def copy(eng, unit, b, x):
        u, n = tp.first[f"kt{b}"] + x, XT * b + x
        if n >= 3:
            eng.wait_ge(kt_read, n - 2)
        tp.wait_filled(eng, u)
        src = tp.bank(u).rearrange("p (k n) -> p k n", k=4)
        if tp.users[u] == "act":
            unit.activation(KT[:, n % 3, :, :], src, ACT.Copy).then_inc(tp.done(u), 1)
        else:
            unit.tensor_copy(KT[:, n % 3, :, :], src).then_inc(tp.done(u), 1)

    return copy


class Ring:

    def __init__(self, banks, filled, emptied_act, emptied_dve):
        self.banks, self.filled = banks, filled
        self.emptied = {"act": emptied_act, "dve": emptied_dve}
        self.users, self.first = [], {}

    def stage(self, name, uses, user):
        self.first[name] = len(self.users)
        self.users += [user] * uses

    def bank(self, m):
        return self.banks[m % len(self.banks)]

    def wait_empty(self, pe, m):
        if m >= len(self.banks):
            self.wait_emptied(pe, m - len(self.banks))

    def wait_emptied(self, eng, m):
        user = self.users[m]
        eng.wait_ge(self.emptied[user], self.users[:m + 1].count(user))

    def wait_filled(self, eng, m):
        eng.wait_ge(self.filled, m + 1)

    def done(self, m):
        return self.emptied[self.users[m]]


def build(nc, t, out):
    ctx = ExitStack()
    with ctx:
        def sem(name):
            return ctx.enter_context(nc.semaphore(name))

        def dram(name, shape, dt=F32):
            return nc.dram_tensor(name, shape, dt, kind="Internal").ap()

        ring_w = SLOTS * SLOT
        HT0 = ring_w
        MIX0 = HT0 + 2 * KD * TOK
        WK0 = MIX0 + TILES * D
        KEPT0 = WK0 + WORK
        STAT0 = KEPT0 + 768 * 2 + 1536 + 2304
        base = -(-nc.sbuf_base // 32) * 32
        arena = ctx.enter_context(nc.sbuf_tensor("arena", [P, STAT0 + 672], F32))
        cst = ctx.enter_context(nc.sbuf_tensor("cst", [P, CONST_W], F32))
        kept, stat = arena[:, KEPT0:STAT0], arena[:, STAT0:STAT0 + 672]
        psum = ctx.enter_context(nc.psum_tensor("psum", [P, 8, CH], F32))

        def c_(name, rows=P):
            a, b = CST[name]
            return cst[0:rows, a:b]

        def shaped(v, shape):
            if len(shape) == 2:
                return v.rearrange("p (a b) -> p a b", a=shape[0])
            if len(shape) == 3:
                return v.rearrange("p (a b c) -> p a b c", a=shape[0], b=shape[1])
            if len(shape) == 4:
                return v.rearrange("p (a b c d) -> p a b c d", a=shape[0], b=shape[1], c=shape[2])
            return v

        def at(start, *shape):
            return shaped(arena[:, start:start + int(np.prod(shape))], shape)

        laid = {}

        def part(start, *shape):
            n = int(np.prod(shape))
            if (start, n) not in laid:
                laid[start, n] = nc.alloc_sbuf_tensor_at(f"part_{start}_{n}", [P, n], F32R, offset=base + 4 * start)
            return shaped(laid[start, n][:, :], shape)

        def parts(start, lo_start, *shape):
            return part(start, *shape), part(lo_start, *shape)

        def slot(n):
            return at((n % SLOTS) * SLOT, SLOT)

        def half_slot(n):
            first = (n % SLOTS) * SLOT
            return at(first, 4, CH), *parts(first + HALF, first, 4, CH)

        hT, hT_lo = parts(HT0, HT0 + KD * TOK, KD, TOK)
        mix = at(MIX0, TILES, D)
        qTs = kept[:, 0:768].rearrange("p (g j n) -> p g j n", g=3, j=4)
        kTs = kept[:, 768:1536].rearrange("p (g j n) -> p g j n", g=3, j=4)
        vs = kept[:, 1536:3072].rearrange("p (g n) -> p g n", g=3)
        oT = kept[:, 3072:5376].rearrange("p (j n) -> p j n", j=4)
        mod = at(WK0, 3, 2, D)
        gain1 = at(WK0 + 4096, D)
        lng, lnb = at(WK0 + 5120, D), at(WK0 + 6144, D)
        x0 = at(WK0 + 7168, TILES, D)
        obT, obT_lo = parts(WK0, KEPT0, KD, TOK)
        sguw = at(WK0 + 12288, H, P)
        sguT = at(WK0 + 13312, H, P)
        sguTs = at(WK0 + 14336, H, NS)
        crow = at(MIX0, D)
        modrow = at(MIX0 + 1024, 2, CH)
        modbias = at(MIX0 + 2048, 2, CH)
        junk1 = at(MIX0 + 3072, D)
        qn = at(MIX0, TILES, CH)
        kn = at(MIX0 + 2560, TILES, CH)
        vn = at(MIX0 + 5120, 4, CH)
        qT = at(MIX0 + 7168, 4, SEQ)
        kT = at(MIX0 + 9216, 4, SEQ)
        scs = [at(MIX0, H, 2 * P), at(MIX0 + 11264, H, 2 * P)]
        pT = at(MIX0 + 13312, 2, H, P)
        abias = at(MIX0 + 15360, 2, H, P)
        oe = at(MIX0 + 17408, 2, OW)
        row_a, rowbias_a = at(MIX0 + 18464, CH), at(MIX0 + 18976, 2, CH)
        KT = at(MIX0, 3, 4, P)
        om = at(MIX0 + 1536, AW)
        pTn = at(MIX0 + 2048, 3, NS)
        ssc = at(MIX0 + 2304, 2, 3, KEYS)
        pTm = at(MIX0 + 3456, 14 * NS)
        Qm = at(MIX0 + 4352, 2, 15 * 256 + 16)
        oin = at(MIX0 + 12064, 4, 3 * OW)
        sbias = at(MIX0 + 18400, 2, 3, KEYS)
        gain = at(WK0 + 6144, D)
        sga = at(WK0 + 7168, TILES, D)
        x1 = sga
        mixT, mixT_lo = hT, hT_lo
        row_b, rowbias_b = at(WK0 + 12288, CH), at(WK0 + 12800, 2, CH)
        gt_tmp = at(WK0 + 14336, CH)
        hrow = at(MIX0, 2, D)
        junk = at(MIX0 + 2048, D)
        h2T = at(HT0, KD, TOK)
        wrt = stat[:, 340:500].rearrange("p (k n) -> p k n", k=KD)
        brt = stat[:, 312:332]
        snm, sden, sf = (stat[:, 512 + 6 * n:518 + 6 * n].rearrange("p (b g) -> p b g", b=2) for n in range(3))
        smin = stat[:, 530:532]
        gp, w1, w2 = (stat[:, 540 + 5 * n:545 + 5 * n] for n in range(3))
        rounds_f = stat[:, 560:561]
        rounds_u = stat[:, 561:562].bitcast(U32)
        tok_u = stat[:, 600:620].bitcast(U32).rearrange("p (k i a) -> p k i a", k=2, i=TILES)
        row_u = stat[:, 570:580].bitcast(U32).rearrange("p (k i) -> p k i", k=2)
        slot_u = stat[:, 580:584].bitcast(U32).rearrange("p (b n) -> p b n", b=2)
        dest_u = stat[:, 584:588].bitcast(U32).rearrange("p (b n) -> p b n", b=2)
        RT0 = MIX0 + 3072

        def rt(start, *shape):
            return at(RT0 + start, *shape)

        lg, eg = rt(0, TILES, 20), rt(100, TILES, 4)
        eq4, cand4, on_g, on_1, on_2 = (rt(120 + 20 * n, TILES, 4) for n in range(5))
        esel, esel2 = rt(220, TILES, 4), rt(240, TILES, 4)
        sc5, id5, e1m, e2m = (rt(260 + 5 * n, TILES) for n in range(4))
        pick, m1, m2, mask, place = (rt(280 + 80 * n, TILES, 16) for n in range(5))
        rowf = rt(680, 2, TILES)
        tmp5 = rt(690, TILES, 4, 4)
        MOE_SLOTS = 6
        TAIL0 = MOE_SLOTS * SLOT
        xg = at(TAIL0, 2, D)
        yb = at(TAIL0 + 2 * D, 2, D)
        acT, acT_lo = parts(TAIL0 + 4 * D, TAIL0 + 4 * D + CH, 4, P)
        sg, ac = at(TAIL0 + 5 * D, CH), at(TAIL0 + 5 * D + CH, CH)
        xgT, xgT_lo = parts(KEPT0, KEPT0 + 2 * D, 2, KD, P)

        def expert_half(n):
            first = n * SLOT
            return at(first, 4, CH), *parts(first + HALF, first, 4, CH)

        yg = at(0, 2, 2, D)
        junk_end = at(2 * SLOT, D)
        cT = part(STAT0, KD, 18)
        sgubT, sgubTs = stat[:, 640:648], stat[:, 648:656]
        ss, rs, lnr = stat[:, 152:157], stat[:, 160:165], stat[:, 168:173]
        bns = stat[:, 176:236].rearrange("p (i n) -> p i n", i=TILES)
        mv = stat[:, 240:250].rearrange("p (i n) -> p i n", i=TILES)
        nmin = stat[:, 256:264]
        fw = stat[:, 264:288].rearrange("p (g h) -> p g h", g=3)
        fd = stat[:, 288:312].rearrange("p (g h) -> p g h", g=3)
        KV_OUTS = [4, 4 + 10, 4 + 10 + 10]

        const_in, x_in, c_in = sem("const_in"), sem("x_in"), sem("c_in")
        slot_in = [sem(f"slot_in{i}") for i in range(SLOTS)]
        mm_filled, mm_act, mm_dve = sem("mm_filled"), sem("mm_act"), sem("mm_dve")
        tp_filled, tp_act, tp_dve = sem("tp_filled"), sem("tp_act"), sem("tp_dve")
        act_step, dve_step, pool_step = sem("act_step"), sem("dve_step"), sem("pool_step")
        silu_done = sem("silu_done")
        hi_done, lo_done = sem("hi_done"), sem("lo_done")
        turned_hi = sem("turned_hi")
        row_out, mod_in = sem("row_out"), sem("mod_in")
        rowbias_in = [sem(f"rowbias_in{n}") for n in range(2)]
        q_zero, gain_used = sem("q_zero"), sem("gain_used")
        bias_zero, mix_out, mix_back = sem("bias_zero"), sem("mix_out"), sem("mix_back")
        bias_in = [sem(f"bias_in{i}") for i in range(2)]
        o_out = [sem(f"o_out{i}") for i in range(2)]
        stat_set = sem("stat_set")
        gain_in, sq_done, var_done, sqrt_done, hn_done = (sem(n) for n in (
            "gain_in", "sq_done", "var_done", "sqrt_done", "hn_done"))
        sgu_in, ln_in, lnvar, lnsqrt, vn_done, vout = (sem(n) for n in (
            "sgu_in", "ln_in", "lnvar", "lnsqrt", "vn_done", "vout"))
        sb_in = [sem(f"sb_in{i}") for i in range(2)]
        q_spread, kt_read, s_max, s_exp, p_ready = (sem(n) for n in (
            "q_spread", "kt_read", "s_max", "s_exp", "p_ready"))
        def pair(name):
            return [sem(f"{name}{n}") for n in range(2)]

        half_in = [sem(f"half_in{n}") for n in range(MOE_SLOTS)]
        idx_in, xg_in, dest_in, y_out = pair("idx_in"), pair("xg_in"), pair("dest_in"), pair("y_out")
        x_filled, x_hi, x_lo, gate_read, gate_filled, sg_done, up_read, up_filled, ac_done = (sem(n) for n in (
            "x_filled", "x_hi", "x_lo", "gate_read", "gate_filled", "sg_done", "up_read", "up_filled", "ac_done"))
        at_filled, at_hi, at_lo, y0_filled, y1_filled, y_act, y_dve, e_hi, e_lo = (sem(n) for n in (
            "at_filled", "at_hi", "at_lo", "y0_filled", "y1_filled", "y_act", "y_dve", "e_hi", "e_lo"))
        sq3, var3, sqrt3, y_done, y_final = (sem(n) for n in ("sq3", "var3", "sqrt3", "y_done", "y_final"))
        yg_in2 = pair("yg_in")
        x2_done = sem("x2_done")
        pool_turn, all_loaded = sem("pool_turn"), sem("all_loaded")
        x1_in, x1_done, h2_done, rt_in, rt_exp_in, rt_exp, mask_done, rows_done, zero_out, tok_out = (
            sem(n) for n in ("x1_in", "x1_done", "h2_done", "rt_in", "rt_exp_in", "rt_exp", "mask_done", "rows_done",
                             "zero_out", "tok_out"))
        sq2, var2, sqrt2 = sem("sq2"), sem("var2"), sem("sqrt2")
        h2_out = [sem(f"h2_out{i}") for i in range(2)]
        kv_out, abias_in, scored, exped, oin_in, lse_dif, lse_exp, oc_done = (
            sem(n) for n in ("kv_out", "abias_in", "scored", "exped",
                             "oin_in", "lse_dif", "lse_exp", "oc_done"))

        mm = Ring([psum[:, b, :] for b in range(6)], mm_filled, mm_act, mm_dve)
        tp = Ring([psum[:, b, :] for b in (6, 7)], tp_filled, tp_act, tp_dve)
        tp.stage("c", 1, "dve")
        mm.stage("ada1", 4 * 3, "dve")
        tp.stage("h", 2 * TILES, "dve")
        mm.stage("v", 2 * TILES, "act")
        tp.stage("sgu", 3, "dve")
        tp.stage("rep", 1, "dve")
        mm.stage("u", 2 * TILES, "act")
        mm.stage("sgu", 2 * TILES, "dve")
        tp.stage("ob", 2 * TILES, "dve")
        mm.stage("gb", 2 * TILES, "act")
        mm.stage("pb", 2 * TILES, "dve")
        GT = [(g, i, [i - 1, i] if g == 0 and i else [i]) for g in range(3) for i in range(4)]
        for g in range(3):
            if g == 0:
                mm.stage("q0", TILES, "act")
            mm.stage(f"k{g}", TILES, "dve")
            mm.stage(f"w{g}", TILES, "act")
            mm.stage(f"row{2 * g}", 1, "dve")
            tp.stage(f"qk{g}", 2 * TILES, "act")
            for i in range(5):
                if i < 4:
                    mm.stage(f"s{g}{i}", 2 * len(GT[4 * g + i][2]), "dve")
                if i == 0:
                    mm.stage(f"row{2 * g + 1}", 1, "dve")
                if i == 4 and g < 2:
                    mm.stage(f"q{g + 1}", TILES, "act")
                if i:
                    tp.stage(f"p{g}{i - 1}", 2 * len(GT[4 * g + i - 1][2]), "act")
                    mm.stage(f"o{g}{i - 1}", 1, "dve")
        KT_USER = ["act", "dve"] * 6 + ["act"]
        for b in range(NB + 2):
            if b < NB:
                tp.first[f"kt{b}"] = len(tp.users)
                tp.users += KT_USER
                mm.stage(f"ss{b}", 3, "dve")
            if b >= 2:
                tp.stage(f"ot{b - 2}", 1, "act")
            if 1 <= b <= NB:
                tp.stage(f"pt{b - 1}", 1, "dve")
                mm.stage(f"so{b - 1}", 1, "dve")
            if 1 <= b <= 4:
                tp.stage(f"o{b - 1}", 1, "act")
        mm.stage("ga", 2 * TILES, "act")
        mm.stage("pa", 2 * TILES, "dve")
        tp.stage("mix", 2 * TILES, "dve")
        mm.stage("wo", 2 * TILES, "dve")
        tp.stage("h2", 2 * TILES, "act")
        mm.stage("rt", TILES, "dve")
        mm.stage("row6", 1, "dve")
        mm.stage("row7", 1, "dve")
        tp.stage("pos", 1, "dve")
        for n in range(8, 12):
            mm.stage(f"row{n}", 1, "dve")

        def row_use(name, n):
            return mm.first[name] + (3 * n - 2 if n else 0)

        def spread_use(name, n, s, count):
            return mm.first[name] + 3 * n + (2 if n < count - 1 else 1) + s

        modp, mods = dram("modp", (2, 3 * D)), dram("mods", (2, NS, 3 * D))
        mixd = dram("mixd", (TOK, D))
        h2d = dram("h2d", (TOK, D))
        yd = dram("yd", (2 * TOK + CAP, D))
        slots_d = dram("slots_d", (E_ALL * EROWS + CAP, 2), U32)
        oscr = [dram(f"oscr{g}", (SEQ, OW)) for g in range(3)]

        def halves(w, j):
            c = w.rearrange("(k p) n -> p k n", p=P)[:, :, j * CH:(j + 1) * CH]
            return [c[:, 0:4, :], c[:, 4:8, :]]

        w_in, w_ada, w_adaf = t["w_in"][0], t["w_ada"][0], t["w_ada_final"]
        ada = [(w_ada, t["b_ada"][0], j) for j in range(12)] + [(w_adaf, t["b_ada_final"], j) for j in range(4)]
        QKV = 3 * 3 * AW
        stream, S0 = [], {}

        slot_last = []

        split = []

        def put(name, last, *srcs):
            S0[name] = len(stream)
            stream.extend(srcs)
            slot_last.extend(last)
            split.extend([False] * len(srcs))

        def put_chunks(name, last, w, js):
            put(name, [m for pair_ in last for m in pair_], *[h for j in js for h in halves(w, j)])
            split[S0[name]:] = [True] * (2 * len(js))

        def projected(name, n=1):
            return [(mm.first[name] + TILES * j, mm.first[name] + TILES * j + TILES - 1) for j in range(n)]

        def put_ada(name, j0, count):
            last = [(row_use(name, n),) * 2 for n in range(count)]
            put(name, [m for pair_ in last for m in pair_], *[h for w, _, j in ada[j0:j0 + count] for h in halves(w, j)])
            split[S0[name]:] = [True] * (2 * count)

        def put_row(n):
            w, _, j = ada[4 + n]
            put_chunks(f"row{n}", [(mm.first[f"row{n}"],) * 2], w, [j])

        put_ada("ada1", 0, 4)
        put_chunks("v", projected("v", 2), w_in, [QKV // CH + 2 + j for j in range(2)])
        put_chunks("u", projected("u", 2), w_in, [QKV // CH + j for j in range(2)])
        put_chunks("gb", projected("gb", 2), w_in, [QKV // CH + 6 + j for j in range(2)])
        put_chunks("pb", projected("pb", 2), t["w_pb"][0], range(2))
        for g in range(3):
            for j, x in enumerate("qkw"):
                put_chunks(f"{x}{g}", projected(f"{x}{g}"), w_in, [3 * j + g])
            for n in (2 * g, 2 * g + 1):
                put_row(n)
        caches = [t[f"cache_kv_w{w}"][0] for w in WINS]

        def keys_of(b, kv, g):
            c = caches[g][b].rearrange("(c r) kv h d -> c r kv (h d)", r=DILS[g])
            return c[:, 0:NC_CLS[g], kv, :]

        def kv_slots(b, kv, last):
            put(f"{'KV'[kv]}{b}", last, [(slice(0, 1), keys_of(b, kv, 0)), (slice(1, 5), keys_of(b, kv, 1))],
                [(slice(0, 8), keys_of(b, kv, 2))])

        for b in range(NB + 1):
            if b < NB:
                f = mm.first[f"ss{b}"]
                kv_slots(b, 0, [f + 1, f + 2])
            if b:
                kv_slots(b - 1, 1, [mm.first[f"so{b - 1}"]] * 2)
        put_chunks("ga", projected("ga", 2), w_in, [QKV // CH + 4 + j for j in range(2)])
        put("pa", [mm.first["pa"] + 9], t["w_pa"][0].rearrange("(j p) n -> p j n", p=P))
        put_chunks("wo", projected("wo", 2), t["w_o"][0], range(2))
        for n in range(6, 12):
            put_row(n)
        N_SLOTS = len(stream)
        slot_total, totals = [], [0] * SLOTS
        for n, src in enumerate(stream):
            totals[n % SLOTS] += 16 * (len(src) if isinstance(src, list) else 1)
            slot_total.append(totals[n % SLOTS])

        halves_to = [sum(split[:n + 1]) for n in range(N_SLOTS)]

        def perm(ap, g, i):
            if g == 0:
                return ap[:, i * P:(i + 1) * P]
            return ap[:, i:SEQ:4]

        def rows_of(ap, g, i):
            return ap[i * P:(i + 1) * P] if g == 0 else ap.rearrange("(s r) n -> r s n", r=4)[i]

        PAIRS = E_ALL // 2

        def rounds_of(eng):
            tp.wait_emptied(eng, tp.first["pos"])
            return eng.value_load(rounds_u[0:1, 0:1], min_val=1, max_val=EROWS // CAP)

        def prime(eng, *sems):
            for s in sems:
                eng.sem_inc(s, 1)

        block = ctx.enter_context(nc.Block())

        @block.sync
        def _(sp):
            def store_row(r):
                mm.wait_emptied(sp, mm.first[f"row{r}"])
                row, cols = row_a if r < 6 else row_b, slice((r % 6) * CH, (r % 6 + 1) * CH)
                sp.dma_start(modp[r // 6:r // 6 + 1, cols], row[0:1, :]).then_inc(row_out, 16)
                sp.dma_start(mods[r // 6].rearrange("(b t) n -> b t n", t=NT)[:, :, cols],
                             row[1:9, :].unsqueeze(1).to_broadcast([NB, NT, CH])).then_inc(row_out, 16)

            for n, src in enumerate(stream):
                if n >= SLOTS:
                    sp.wait_ge(mm_filled, slot_last[n - SLOTS] + 1)
                if split[n]:
                    sp.dma_start(half_slot(n)[0], src).then_inc(slot_in[n % SLOTS], 16)
                else:
                    for part_, a in src if isinstance(src, list) else [(slice(0, src.shape[1]), src)]:
                        dst = slot(n).rearrange("p (k n) -> p k n", n=a.shape[-1])[:, part_, :]
                        sp.dma_start(dst, a).then_inc(slot_in[n % SLOTS], 16)
                for r in range(12):
                    if n == S0[f"row{r}"] + SLOTS + 1:
                        store_row(r)
            rounds = rounds_of(sp)
            store_row(10)
            store_row(11)
            for n in range(N_SLOTS - SLOTS, N_SLOTS):
                sp.wait_ge(mm_filled, slot_last[n] + 1)

            def load(w, e, at_, h):
                src = w[bass.ds(e, 1)] if at_ < 4 else w[bass.ds(e, 1), :, h * CH:(h + 1) * CH]
                src = src.rearrange("a (k p) n -> p (a k) n", p=P)
                src = src[:, 4 * h:4 * h + 4, :] if at_ < 4 else src
                sp.dma_start(expert_half(at_ + h)[0], src).then_inc(half_in[at_ + h], 16)

            for h in range(2):
                load(t["w_gate"][0], 0, 0, h)
            with sp.Fori(0, rounds * PAIRS) as it:
                def pair_loads(w, at_, read, n, e):
                    for h in range(2):
                        sp.wait_ge(read[h], n)
                        load(w, e, at_, h)

                e = (it % PAIRS) * 2
                for par in range(2):
                    n = it * 2 + par
                    pair_loads(t["w_up"][0], 2, (up_read, up_filled), n + 1, e + par)
                    pair_loads(t["w_down"][0], 4, (y0_filled, y1_filled), n + 1, e + par)
                    pair_loads(t["w_gate"][0], 0, (gate_read, gate_filled), n + 1, e + 1 if par == 0 else ((it + 1) % PAIRS) * 2)
            for h in range(2):
                sp.wait_ge(half_in[h], rounds * (32 * PAIRS) + 16)
            sp.sem_inc(all_loaded, 1)

        @block.gpsimd
        def _(pool):
            pool.dma_start(crow[0:1, :], t["c_prompt"]).then_inc(c_in, 16)
            pool.dma_start(crow[1:1 + NB, :], t["c_sample"]).then_inc(c_in, 16)
            pool.dma_start(cst[:, :], t["consts"]).then_inc(const_in, 16)
            pool.dma_start(x0[:, 0:4, :], t["x_prompt"][0].rearrange("(i p) d -> p i d", p=P)).then_inc(x_in, 16)
            pool.dma_start(x0[0:NS, 4, :], t["x_sample"].rearrange("b t d -> (b t) d")).then_inc(x_in, 16)
            pool.dma_start(gain1, t["norm1_g"].partition_broadcast(P)).then_inc(gain_in, 16)

            def bias_rows(name, buf, j0, count):
                pool.memset(buf[0:18, :, :], 0.0).then_inc(bias_zero, 1)
                pool.wait_ge(bias_zero, 1)
                for n in range(count):
                    if n >= 2:
                        mm.wait_emptied(pool, row_use(name, n - 2))
                    load_bias(buf[0:9, n % 2, :], j0 + n, bias_in[n % 2])

            def load_bias(dst, j, signal):
                _, b, col = ada[j]
                pool.dma_start(dst, b[col * CH:(col + 1) * CH].rearrange("(a n) -> a n", a=1).partition_broadcast(9)
                               ).then_inc(signal, 16)

            def row_biases(r):
                for n in (r, r + 1):
                    if n % 6 >= 2:
                        mm.wait_emptied(pool, mm.first[f"row{n - 2}"])
                    load_bias((rowbias_a if n < 6 else rowbias_b)[0:9, n % 2, :], 4 + n, rowbias_in[n % 2])

            def load_modulation(norm):
                pool.wait_ge(row_out, 32 * 6 * (norm + 1))
                for v, which in enumerate((2, 0, 1)):
                    cols = slice(v * D, (v + 1) * D)
                    pool.dma_start(mod[:, which, 0, :], modp[norm:norm + 1, cols].partition_broadcast(P)).then_inc(mod_in, 16)
                    pool.dma_start(mod[0:NS, which, 1, :], mods[norm, :, cols]).then_inc(mod_in, 16)

            bias_rows("ada1", modbias, 0, 4)
            pool.dma_start(sguw, t["sgu_w"][0].rearrange("g t s -> t g s")).then_inc(sgu_in, 16)
            pool.dma_start(stat[0:H, 384:512], t["sgu_b"][0]).then_inc(sgu_in, 16)
            pool.dma_start(lng, t["sgu_ln_g"].partition_broadcast(P)).then_inc(ln_in, 16)
            pool.dma_start(lnb, t["sgu_ln_b"].partition_broadcast(P)).then_inc(ln_in, 16)
            pool.wait_ge(vn_done, TILES)
            pool.dma_start(out["sgu_v"], mix[0:NS, 4, :]).then_inc(vout, 16)
            for i in range(TILES):
                mm.wait_emptied(pool, mm.first["pb"] + TILES + i)
                pool.dma_start(mixd[i * P:i * P + ROWS[i], :], mix[0:ROWS[i], i, :]).then_inc(mix_out, 16)
            for g in range(3):
                if g == 0:
                    pool.wait_ge(mm_filled, mm.first["pb"] + 10)
                row_biases(2 * g)
                for kind in ((0, 1), (2,), (3,))[g]:
                    if kind < 2:
                        if kind == 0:
                            pool.wait_ge(mm_filled, mm.first["pb"] + 10)
                    else:
                        pool.wait_ge(scored, 4 * g)
                    pool.dma_start(abias[:, kind if kind < 2 else 1, :, :],
                                   t["pbias"][kind]).then_inc(abias_in, 16)
                mm.wait_emptied(pool, mm.first[f"k{g}"] + TILES - 1)
                mm.wait_emptied(pool, mm.first[f"w{g}"] + TILES - 1)
                kvp, kvs = out["kvp"][g], out["kvs"][g]
                for part, src in ((0, kn), (1, vn)):
                    for i in range(4):
                        if g == 0 and i < 3:
                            continue
                        rows = kvp if g == 0 else rows_of(kvp, g, i)
                        pool.dma_start(rows[:, part * AW:(part + 1) * AW], src[:, i, :]).then_inc(kv_out, 16)
                pool.dma_start(kvs[:, 0:AW], kn[0:NS, 4, :]).then_inc(kv_out, 16)
                pool.dma_start(kvs[:, AW:2 * AW], vs[0:NS, g, :]).then_inc(kv_out, 16)
                for i in range(4):
                    mm.wait_emptied(pool, mm.first[f"o{g}{i}"])
                    pool.dma_start(rows_of(oscr[g], g, i), oe[:, i % 2, :]).then_inc(o_out[i % 2], 16)
            for o in o_out:
                pool.wait_ge(o, 16 * 6)
            for g in range(3):
                pool.dma_start(oin[:, :, g * OW:(g + 1) * OW], oscr[g].rearrange("(i p) n -> p i n", p=P)).then_inc(oin_in, 16)
            pool.memset(Qm[:, 1, :], 0.0).then_inc(q_zero, 1)
            pool.wait_ge(row_out, 32 * 6)
            for b in range(NB):
                if b >= 2:
                    mm.wait_emptied(pool, mm.first[f"ss{b - 2}"] + 2)
                pool.dma_start(sbias[0:NS, b % 2, :, :], t["sbias"][b]).then_inc(sb_in[b % 2], 16)
            mm.wait_emptied(pool, mm.first[f"ss{NB - 1}"] + 2)
            pool.dma_start(gain, t["norm2_g"].partition_broadcast(P)).then_inc(gain_in, 16)
            pool.dma_start(wrt[:, :, 0:4], t["w_route_group"][0].rearrange("(k p) n -> p k n", p=P)).then_inc(rt_in, 16)
            for g in range(4):
                pool.dma_start(wrt[:, :, 4 + 4 * g:8 + 4 * g],
                               t["w_route_expert"][0, g].rearrange("(k p) n -> p k n", p=P)).then_inc(rt_in, 16)
            pool.dma_start(brt[:, 0:4], t["b_route_group"].partition_broadcast(P)).then_inc(rt_in, 16)
            pool.dma_start(brt[:, 4:20], t["b_route_expert"].rearrange("a g e -> a (g e)").partition_broadcast(P)).then_inc(rt_in, 16)
            tp.wait_filled(pool, tp.first[f"ot{NB - 1}"])
            pool.dma_start(mix[:, 0:4, :], mixd[0:SEQ].rearrange("(i p) n -> p i n", p=P)).then_inc(mix_back, 16)
            pool.dma_start(mix[0:NS, 4, :], mixd[SEQ:TOK]).then_inc(mix_back, 16)
            load_modulation(0)
            mm.wait_emptied(pool, mm.first["pa"] + 9)
            pool.dma_start(x1[:, 0:4, :], t["x_prompt"][0].rearrange("(i p) d -> p i d", p=P)).then_inc(x1_in, 16)
            pool.dma_start(x1[0:NS, 4, :], t["x_sample"].rearrange("b t d -> (b t) d")).then_inc(x1_in, 16)
            for i in range(TILES):
                pool.wait_ge(h2_done, i + 1)
                pool.dma_start(h2d[i * P:i * P + ROWS[i], :], hrow[0:ROWS[i], i % 2, :]).then_inc(h2_out[i % 2], 16)
            for r in (6, 8, 10):
                row_biases(r)
            pool.wait_ge(gain_used, 1)
            pool.dma_start(gain, t["normf_g"].rearrange("(a n) -> a n", a=1).partition_broadcast(P)).then_inc(gain_in, 16)
            pool.dma_start(slots_d, t["empty_slots"]).then_inc(zero_out, 16)
            pool.dma_start(tok_u.rearrange("p k i a -> p (k i a)"), t["token_places"]).then_inc(zero_out, 16)
            pool.wait_ge(zero_out, 32)
            pool.wait_ge(rows_done, 1)
            for k in range(2):
                for i in range(TILES):
                    n = ROWS[i]
                    pool.indirect_dma_start(slots_d, bass.IndirectOffsetOnAxis(ap=row_u[0:n, k, i:i + 1], axis=0),
                                            tok_u[0:n, k, i, :], None).then_inc(tok_out, 16)
            pool.wait_ge(tok_out, 16 * 2 * TILES)
            for n in range(2):
                pool.wait_ge(h2_out[n], 16 * (3 - n))
            rounds = rounds_of(pool)

            def waited():
                pool.sem_inc(pool_turn, 1)

            def fetch(it, par, turned):
                row = ((it % PAIRS) * 2 + par) * EROWS + (it // PAIRS) * CAP
                pool.dma_start(slot_u[:, par, :], slots_d[bass.ds(row, CAP), :]).then_inc(idx_in[par], 16)
                pool.wait_ge(idx_in[par], it * 16 + 16)
                if turned is not None:
                    pool.wait_ge(x_filled, turned)
                waited()
                pool.indirect_dma_start(xg[:, par, :], None, h2d, bass.IndirectOffsetOnAxis(
                    ap=slot_u[:, par, 0:1], axis=0)).then_inc(xg_in[par], 16)

            def scatter(it, par):
                row = ((it % PAIRS) * 2 + par) * EROWS + (it // PAIRS) * CAP
                pool.dma_start(dest_u[:, par, :], slots_d[bass.ds(row, CAP), :]).then_inc(dest_in[par], 16)
                pool.wait_ge(dest_in[par], it * 16 + 16)
                pool.wait_ge(y_act, it * 2 + par + 2)
                pool.wait_ge(y_dve, it * 2 + par + 2)
                pool.wait_ge(y_out[1 - par], it * 16 + 16 if par == 0 else it * 16 + 32)
                waited()
                pool.indirect_dma_start(yd, bass.IndirectOffsetOnAxis(ap=dest_u[:, par, 1:2], axis=0),
                                        yb[:, par, :], None).then_inc(y_out[par], 16)

            for par in range(2):
                pool.dma_start(yd[2 * TOK + par:2 * TOK + par + 1, :], h2d[par:par + 1, :]).then_inc(y_out[par], 16)
            fetch(0, 0, None)
            fetch(0, 1, None)
            load_modulation(1)
            with pool.Fori(0, rounds * PAIRS) as it:
                for par in range(2):
                    pool.wait_ge(xg_in[par], it * 16 + 16)
                    fetch(it + 1, par, it * 4 + 2 * par + 2)
                    scatter(it, par)
            for par in range(2):
                pool.wait_ge(xg_in[par], rounds * (PAIRS * 16) + 16)
                pool.wait_ge(y_out[par], rounds * (PAIRS * 16) + 16)
            waited()
            for i in range(TILES):
                n = ROWS[i]
                if i >= 2:
                    pool.wait_ge(x2_done, i - 1)
                pool.dma_start(yg[0:n, i % 2, :, :], yd[2 * i * P:2 * (i * P + n), :].rearrange("(p k) n -> p k n", k=2)
                               ).then_inc(yg_in2[i % 2], 16)
            pool.wait_ge(kv_out, 16 * KV_OUTS[-1])
            pool.wait_ge(vout, 16)
            for i in range(TILES):
                pool.wait_ge(y_done, i + 1)
                dst = out["y_prompt"][i * P:(i + 1) * P, :] if i < 4 else out["y_sample"]
                pool.dma_start(dst, x1[0:ROWS[i], i, :]).then_inc(y_final, 16)
            pool.wait_ge(y_final, 16 * TILES)

        @block.tensor
        def _(pe):
            used = [0]

            def slot_wait(n):
                pe.wait_ge(slot_in[n % SLOTS], slot_total[n])

            def transposes(first, u, n, pieces):
                tp.wait_empty(pe, first + u)
                bank = tp.bank(first + u)
                for k, a in enumerate(pieces):
                    ins = nc.tensor.transpose(bank[0:a.shape[-1], k * n:k * n + a.shape[0]], a,
                                              c_("ident", a.shape[0])[:, 0:a.shape[0]])
                ins.then_inc(tp_filled, 1)

            def half_wait(n):
                pe.wait_ge(lo_done, halves_to[n])

            last_product = [None]

            def three_passes(out_, hi, lo, w_hi, w_lo, start, stop):
                nc.tensor.matmul(out_, hi, w_hi, start=start, stop=False)
                nc.tensor.matmul(out_, hi, w_lo, start=False, stop=False)
                last_product[0] = nc.tensor.matmul(out_, lo, w_hi, start=False, stop=stop)

            def tally(signal):
                last_product[0].then_inc(signal, 1)

            def later_row(n):
                m = mm.first[f"row{n}"]
                mm.wait_empty(pe, m)
                for half in range(2):
                    half_wait(S0[f"row{n}"] + half)
                    _, w_hi, w_lo = half_slot(S0[f"row{n}"] + half)
                    for k in range(4):
                        c = cT[:, 4 * half + k, :]
                        three_passes(mm.bank(m)[0:9, :], c[:, 0:9], c[:, 9:18], w_hi[:, k, :], w_lo[:, k, :],
                                     half == 0 and k == 0, half == 1 and k == 3)
                tally(mm_filled)

            def project(name, lhs, j, g=0):
                for half in range(2):
                    n = S0[name] + 2 * j + half
                    half_wait(n)
                    _, w_hi, w_lo = half_slot(n)
                    for i in range(TILES):
                        m = mm.first[name] + TILES * j + i
                        if half == 0:
                            mm.wait_empty(pe, m)
                        for k in range(4):
                            hi, lo = ((x[:, 4 * half + k, SEQ:TOK] if i == 4 else perm(x[:, 4 * half + k, :], g, i))
                                      for x in lhs)
                            last = half == 1 and k == 3
                            three_passes(mm.bank(m)[0:ROWS[i], :], hi, lo, w_hi[:, k, :], w_lo[:, k, :],
                                         half == 0 and k == 0, last)
                        if half == 1:
                            tally(mm_filled)

            def modulation(name, rows, count):
                def row(n):
                    m = row_use(name, n)
                    mm.wait_empty(pe, m)
                    for half in range(2):
                        half_wait(S0[name] + 2 * n + half)
                        _, w_hi, w_lo = half_slot(S0[name] + 2 * n + half)
                        for k in range(4):
                            first, last = half == 0 and k == 0, half == 1 and k == 3
                            c = cT[:, 4 * half + k, :]
                            nc.tensor.matmul(mm.bank(m)[0:18, :], c, w_hi[:, k, :], start=first, stop=False)
                            ins = nc.tensor.matmul(mm.bank(m)[0:18, :], c, w_lo[:, k, :], start=False, stop=last)
                    ins.then_inc(mm_filled, 1)

                def spread(n):
                    mm.wait_emptied(pe, row_use(name, n))
                    for s in range(2):
                        m = spread_use(name, n, s, count)
                        mm.wait_empty(pe, m)
                        w = (P, NS)[s]
                        nc.tensor.matmul(mm.bank(m)[0:w, :], c_("selmod", 18)[:, s * P:s * P + w], rows[0:18, n % 2, :],
                                         start=True, stop=True).then_inc(mm_filled, 1)

                row(0)
                for n in range(count):
                    if n + 1 < count:
                        row(n + 1)
                    spread(n)

            pe.wait_ge(const_in, 16)
            pe.wait_ge(silu_done, 1)
            transposes(tp.first["c"], 0, 9, [crow[0:9, k * P:(k + 1) * P] for k in range(KD)])
            tp.wait_emptied(pe, tp.first["c"])
            modulation("ada1", modrow, 4)
            H_PARTS = (hT, hT_lo)
            for i in range(TILES):
                pe.wait_ge(hn_done, i + 1)
                for half in range(2):
                    transposes(tp.first["h"], 2 * i + half, ROWS[i],
                               [x0[0:ROWS[i], i, (4 * half + k) * P:(4 * half + k + 1) * P] for k in range(4)])
            tp.wait_emptied(pe, tp.first["h"] + 2 * TILES - 1)
            for j in range(2):
                project("v", H_PARTS, j)
            pe.wait_ge(sgu_in, 32)
            for half in range(2):
                transposes(tp.first["sgu"], half, P, [sguw[:, 4 * half + k, :] for k in range(4)])
            transposes(tp.first["sgu"], 2, H, [stat[0:H, 384:512]])
            tp.wait_emptied(pe, tp.first["sgu"] + 2)
            m = tp.first["rep"]
            tp.wait_empty(pe, m)
            nc.tensor.matmul(tp.bank(m)[0:NS, 0:NS], c_("rep", NT), sguT[0:NT, :, 0:NT], start=True, stop=True)
            nc.tensor.matmul(tp.bank(m)[0:NS, NS:NS + H], c_("rep", NT), sgubT[0:NT, :],
                             start=True, stop=True).then_inc(tp_filled, 1)
            for j in range(2):
                project("u", H_PARTS, j)
            tp.wait_emptied(pe, tp.first["rep"])
            for i in range(TILES):
                pe.wait_ge(vn_done, i + 1)
                for half in range(2):
                    m = mm.first["sgu"] + 2 * i + half
                    mm.wait_empty(pe, m)
                    for k in range(4):
                        g = 4 * half + k
                        n = ROWS[i]
                        ins = nc.tensor.matmul(mm.bank(m)[0:n, k * P:(k + 1) * P],
                                               (sguT[:, g, :] if i < 4 else sguTs[0:NS, g, :]),
                                               mix[0:n, i, g * P:(g + 1) * P], start=True, stop=True)
                    ins.then_inc(mm_filled, 1)
            project("gb", H_PARTS, 0)
            for i in range(TILES):
                mm.wait_emptied(pe, mm.first["sgu"] + 2 * i + 1)
                for half in range(2):
                    transposes(tp.first["ob"], 2 * i + half, ROWS[i],
                               [x0[0:ROWS[i], i, (4 * half + k) * P:(4 * half + k + 1) * P] for k in range(4)])
            project("gb", H_PARTS, 1)
            tp.wait_emptied(pe, tp.first["ob"] + 9)
            for j in range(2):
                project("pb", (obT, obT_lo), j)
            def tile_scores(g, i, keys):
                for kk, kt in enumerate(keys):
                    for par in range(2):
                        m = mm.first[f"s{g}{i}"] + 2 * kk + par
                        mm.wait_empty(pe, m)
                        for j in range(4):
                            ins = nc.tensor.matmul(mm.bank(m)[:, j * P:(j + 1) * P],
                                                   qT[64 * par:64 * par + 64, j, i * P:(i + 1) * P],
                                                   kT[64 * par:64 * par + 64, j, kt * P:(kt + 1) * P],
                                                   start=True, stop=True)
                        ins.then_inc(mm_filled, 1)

            def tile_values(g, i, keys):
                nk = len(keys)
                pe.wait_ge(exped, 4 * g + i + 1)
                for kk in range(nk):
                    for par in range(2):
                        transposes(tp.first[f"p{g}{i}"], 2 * kk + par, P,
                                   [scs[i % 2][:, 4 * par + j, kk * P:(kk + 1) * P] for j in range(4)])
                tp.wait_emptied(pe, tp.first[f"p{g}{i}"] + 2 * nk - 1)
                if i == 0:
                    mm.wait_emptied(pe, mm.first[f"w{g}"] + TILES - 1)
                m = mm.first[f"o{g}{i}"]
                mm.wait_empty(pe, m)
                for hp in range(H):
                    h = head_of(hp)
                    for kk, kt in enumerate(keys):
                        ins = nc.tensor.matmul(mm.bank(m)[:, h * DH:(h + 1) * DH], pT[:, kk, hp, :],
                                               vn[:, kt, h * DH:(h + 1) * DH], start=(kk == 0), stop=(kk == nk - 1))
                ins.then_inc(mm_filled, 1)

            project("q0", H_PARTS, 0)
            for g in range(3):
                project(f"k{g}", H_PARTS, 0, g=g)
                project(f"w{g}", H_PARTS, 0, g=g)
                later_row(2 * g)
                for j, src in enumerate((qn, kn)):
                    mm.wait_emptied(pe, mm.first[f"{'qk'[j]}{g}"] + TILES - 1)
                    for i in range(TILES):
                        transposes(tp.first[f"qk{g}"], TILES * j + i, ROWS[i],
                                   [src[0:ROWS[i], i, k * P:(k + 1) * P] for k in range(4)])
                tp.wait_emptied(pe, tp.first[f"qk{g}"] + 2 * TILES - 1)
                tiles = GT[4 * g:4 * g + 4]
                tile_scores(*tiles[0])
                later_row(2 * g + 1)
                for i in range(1, 4):
                    tile_scores(*tiles[i])
                    tile_values(*tiles[i - 1])
                if g < 2:
                    project(f"q{g + 1}", H_PARTS, 0, g=g + 1)
                tile_values(*tiles[3])

            def key_tile(b, x):
                n = S0[f"K{b}"] + (x >= CLS0[2])
                return slot(n).rearrange("p (k n) -> p k n", n=AW)[:, x - (CLS0[2] if x >= CLS0[2] else 0), :], n

            def turn_keys(b, x):
                tile, n = key_tile(b, x)
                if x in (0, CLS0[2]):
                    slot_wait(n)
                transposes(tp.first[f"kt{b}"], x, P, [tile[:, j * P:(j + 1) * P] for j in range(4)])

            def scores(b):
                pe.wait_ge(q_spread, b + 1)
                turn_keys(b, 0)
                for x in range(XT):
                    g = 0 if x < CLS0[1] else 1 if x < CLS0[2] else 2
                    if x + 1 < XT:
                        turn_keys(b, x + 1)
                    m = mm.first[f"ss{b}"] + g
                    if x == CLS0[g]:
                        mm.wait_empty(pe, m)
                    tp.wait_emptied(pe, tp.first[f"kt{b}"] + x)
                    for j in range(4):
                        ins = nc.tensor.matmul(mm.bank(m)[0:NS, 0:P], Qm[:, b % 2, x * 256 + j * NS:x * 256 + (j + 1) * NS],
                                               KT[:, (XT * b + x) % 3, j, :], start=(x == CLS0[g] and j == 0),
                                               stop=(x == CLS0[g] + NC_CLS[g] - 1 and j == 3))
                    ins.then_inc(kt_read, 1)
                    if x == CLS0[g] + NC_CLS[g] - 1:
                        whole = (0, 13, 14)[g]
                        for j in range(4):
                            ins = nc.tensor.matmul(mm.bank(m)[0:NS, P:KEYS],
                                                   Qm[:, b % 2, whole * 256 + j * NS:whole * 256 + (j + 1) * NS],
                                                   kTs[:, g, j, :], start=(j == 0), stop=(j == 3))
                        ins.then_inc(mm_filled, 1)

            def attend(b):
                u = tp.first[f"pt{b}"]
                pe.wait_ge(p_ready, b + 1)
                tp.wait_empty(pe, u)
                bank = tp.bank(u)
                for g in range(3):
                    nc.tensor.transpose(bank[:, g * NS:(g + 1) * NS], ssc[0:NS, b % 2, g, 0:P],
                                        c_("ident", NS)[:, 0:NS])
                for g in range(3):
                    ins = nc.tensor.transpose(bank[0:NS, (3 + g) * NS:(4 + g) * NS], ssc[0:NS, b % 2, g, P:KEYS],
                                              c_("ident", NS)[:, 0:NS])
                ins.then_inc(tp_filled, 1)
                m = mm.first[f"so{b}"]
                mm.wait_empty(pe, m)
                tp.wait_emptied(pe, u)
                for g in range(3):
                    nc.tensor.matmul(mm.bank(m)[0:NS, :], pTn[0:NS, g, :], vs[0:NS, g, :], start=(g == 0), stop=False)
                for x in range(XT):
                    n = S0[f"V{b}"] + (x >= CLS0[2])
                    if x in (0, CLS0[2]):
                        slot_wait(n)
                    tile = slot(n).rearrange("p (k n) -> p k n", n=AW)[:, x - (CLS0[2] if x >= CLS0[2] else 0), :]
                    ins = nc.tensor.matmul(mm.bank(m)[0:NS, :], pTm[:, x * NS:(x + 1) * NS], tile, start=False,
                                           stop=(x == XT - 1))
                ins.then_inc(mm_filled, 1)

            def gather_heads(b):
                u = tp.first[f"ot{b}"]
                mm.wait_emptied(pe, mm.first[f"so{b}"])
                tp.wait_empty(pe, u)
                for j in range(4):
                    ins = nc.tensor.matmul(tp.bank(u)[:, j * NT:(j + 1) * NT], om[0:NS, j * P:(j + 1) * P],
                                           c_("seltok", NS), start=True, stop=True)
                ins.then_inc(tp_filled, 1)

            for b in range(NB + 2):
                if b < NB:
                    scores(b)
                if b >= 2:
                    gather_heads(b - 2)
                if 1 <= b <= NB:
                    attend(b - 1)
                if 1 <= b <= 4:
                    pe.wait_ge(oc_done, b)
                    transposes(tp.first[f"o{b - 1}"], 0, P, [oin[:, b - 1, k * P:(k + 1) * P] for k in range(4)])
            for j in range(2):
                project("ga", H_PARTS, j)
            slot_wait(S0["pa"])
            tp.wait_emptied(pe, tp.first[f"ot{NB - 1}"])
            wpa = slot(S0["pa"]).rearrange("p (j n) -> p j n", j=4)
            for c in range(2):
                for i in range(TILES):
                    m = mm.first["pa"] + TILES * c + i
                    mm.wait_empty(pe, m)
                    for j in range(4):
                        ins = nc.tensor.matmul(mm.bank(m)[0:ROWS[i], :], oT[:, j, i * P:i * P + ROWS[i]],
                                               wpa[:, j, c * CH:(c + 1) * CH], start=(j == 0), stop=(j == 3))
                    ins.then_inc(mm_filled, 1)
            mm.wait_emptied(pe, mm.first["pa"] + 9)
            for i in range(TILES):
                for half in range(2):
                    transposes(tp.first["mix"], 2 * i + half, ROWS[i],
                               [mix[0:ROWS[i], i, (4 * half + k) * P:(4 * half + k + 1) * P] for k in range(4)])
            tp.wait_emptied(pe, tp.first["mix"] + 9)
            for j in range(2):
                project("wo", (mixT, mixT_lo), j)
            for i in range(TILES):
                pe.wait_ge(h2_done, i + 1)
                for half in range(2):
                    transposes(tp.first["h2"], 2 * i + half, ROWS[i],
                               [hrow[0:ROWS[i], i % 2, (4 * half + k) * P:(4 * half + k + 1) * P] for k in range(4)])
            pe.wait_ge(rt_in, 16 * 6)
            for i in range(TILES):
                m = mm.first["rt"] + i
                mm.wait_empty(pe, m)
                tp.wait_emptied(pe, tp.first["h2"] + 2 * i + 1)
                for k in range(KD):
                    ins = nc.tensor.matmul(mm.bank(m)[0:ROWS[i], 0:20], h2T[:, k, i * P:i * P + ROWS[i]], wrt[:, k, :],
                                           start=(k == 0), stop=(k == KD - 1))
                ins.then_inc(mm_filled, 1)
            later_row(6)
            later_row(7)
            m = tp.first["pos"]
            pe.wait_ge(mask_done, 1)
            tp.wait_empty(pe, m)
            for i in range(TILES + 1):
                for e in range(min(i, TILES - 1) + 1 if i < TILES else TILES):
                    own_tile = e == i
                    last = e == min(i, TILES - 1)
                    ins = nc.tensor.matmul(tp.bank(m)[:, 16 * i:16 * i + 16], c_("before") if own_tile else c_("ones"),
                                           mask[:, e, :], start=(e == 0), stop=last)
            ins.then_inc(tp_filled, 1)
            for n in range(8, 12):
                later_row(n)
            rounds = rounds_of(pe)
            X, GATE, UP, AT, Y = (psum[:, 0, :], psum[:, 1, :]), psum[:, 2, :], psum[:, 3, :], psum[:, 4, :], (
                psum[:, 5, :], psum[:, 6, :])
            ident = c_("ident")
            mm.wait_emptied(pe, len(mm.users) - 1)
            tp.wait_emptied(pe, len(tp.users) - 1)

            def turn_tokens(par, n, it, c):
                if c == 0:
                    pe.wait_ge(xg_in[par], it * 16 + 16)
                if n is not None:
                    pe.wait_ge(x_lo, n * 2 + c - 1)
                for k in range(4):
                    ins = nc.tensor.transpose(X[c][:, k * P:(k + 1) * P],
                                              xg[:, par, (4 * c + k) * P:(4 * c + k + 1) * P], ident)
                ins.then_inc(x_filled, 1)

            def hidden(par, bank, at_, split_to, read, filled):
                for h in range(2):
                    pe.wait_ge(e_lo, split_to + h)
                    _, w_hi, w_lo = expert_half(at_ + h)
                    for k in range(4):
                        three_passes(bank, xgT[:, par, 4 * h + k, :], xgT_lo[:, par, 4 * h + k, :], w_hi[:, k, :],
                                     w_lo[:, k, :], h == 0 and k == 0, h == 1 and k == 3)
                    tally((read, filled)[h])

            def gate(par, n, split_to):
                pe.wait_ge(x_lo, n * 2 + 2)
                hidden(par, GATE, 0, split_to, gate_read, gate_filled)

            def up(par, split_to):
                hidden(par, UP, 2, split_to, up_read, up_filled)

            def turn_hidden(n):
                pe.wait_ge(ac_done, n + 1)
                for k in range(4):
                    ins = nc.tensor.transpose(AT[:, k * P:(k + 1) * P], ac[:, k * P:(k + 1) * P], ident)
                ins.then_inc(at_filled, 1)

            def down(n, split_to):
                pe.wait_ge(at_lo, n + 1)
                for c in range(2):
                    pe.wait_ge(e_lo, split_to + c)
                    pe.wait_ge((y_act, y_dve)[c], n + 1)
                    _, w_hi, w_lo = expert_half(4 + c)
                    for k in range(4):
                        three_passes(Y[c], acT[:, k, :], acT_lo[:, k, :], w_hi[:, k, :], w_lo[:, k, :], k == 0, k == 3)
                    tally((y0_filled, y1_filled)[c])

            prime(pe, up_read, up_filled, y0_filled, y1_filled)
            for c in range(2):
                turn_tokens(0, None, 0, c)
            with pe.Fori(0, rounds * PAIRS) as it:
                for par in range(2):
                    n, after = it * 2 + par, (1, it) if par == 0 else (0, it + 1)
                    gate(par, n, n * 6 + 1)
                    up(par, n * 6 + 3)
                    turn_tokens(after[0], n + 1, after[1], 0)
                    turn_hidden(n)
                    turn_tokens(after[0], n + 1, after[1], 1)
                    down(n, n * 6 + 5)

        @block.scalar
        def _(act):
            steps = [0]

            def own(ins):
                steps[0] += 1
                ins.then_inc(act_step, 1)
                act.wait_ge(act_step, steps[0])

            def empty(ring, m, dst, n, func, scale=1.0, cols=CH, src=None):
                ring.wait_filled(act, m)
                nc.scalar.activation(dst, ring.bank(m)[0:n, 0:cols] if src is None else src, func,
                                     scale=scale).then_inc(ring.done(m), 1)

            parted = [0]

            def split_to(last):
                for n in range(parted[0], min(last + 1, N_SLOTS)):
                    if split[n]:
                        raw, hi, _ = half_slot(n)
                        act.wait_ge(slot_in[n % SLOTS], slot_total[n])
                        nc.scalar.activation(hi, raw, ACT.Copy).then_inc(hi_done, 1)
                    parted[0] = n + 1

            def turn_hi(first, u, n, dst):
                tp.wait_filled(act, first + u)
                nc.scalar.activation(dst, tp.bank(first + u)[:, 0:4 * n].rearrange("p (k n) -> p k n", k=4),
                                     ACT.Copy).then_inc(turned_hi, 1)

            def turn_in(first, u, n, dst):
                m = first + u
                empty(tp, m, dst, P, ACT.Copy, src=tp.bank(m)[:, 0:4 * n].rearrange("p (k n) -> p k n", k=4))

            key_copy = copy_keys(tp, KT, kt_read)

            act.wait_ge(c_in, 32)
            nc.scalar.activation(crow[0:9, :], crow[0:9, :], ACT.Silu).then_inc(silu_done, 1)
            split_to(3)
            act.wait_ge(x_in, 32)
            act.wait_ge(stat_set, 1)
            for i in range(TILES):
                n = ROWS[i]
                if i:
                    act.wait_ge(sq_done, i)
                nc.scalar.activation(junk1[0:n, :], x0[0:n, i, :], ACT.Square,
                                     accum_out=ss[0:n, i:i + 1]).then_inc(sq_done, 1)
            split_to(S0["v"] + 1)
            act.wait_ge(var_done, 1)
            nc.scalar.activation(rs, rs, ACT.Sqrt).then_inc(sqrt_done, 1)
            split_to(S0["v"] + 3)
            for i in range(TILES):
                for half in range(2):
                    turn_hi(tp.first["h"], 2 * i + half, ROWS[i],
                            hT[:, 4 * half:4 * half + 4, i * P:i * P + ROWS[i]])
            for j in range(2):
                split_to(S0["v"] + 2 * j + 3)
                for i in range(TILES):
                    n = ROWS[i]
                    empty(mm, mm.first["v"] + TILES * j + i, mix[0:n, i, j * CH:(j + 1) * CH], n, ACT.Gelu_apprx_tanh)
            split_to(S0["u"] + 3)
            act.wait_ge(lnvar, 1)
            nc.scalar.activation(lnr, lnr, ACT.Sqrt).then_inc(lnsqrt, 1)
            for j in range(2):
                split_to(S0["u"] + 2 * j + 3)
                for i in range(TILES):
                    n = ROWS[i]
                    empty(mm, mm.first["u"] + TILES * j + i, x0[0:n, i, j * CH:(j + 1) * CH], n, ACT.Gelu_apprx_tanh)
            act.wait_ge(vout, 16)
            for j in range(2):
                split_to(S0["gb"] + 2 * j + 3)
                for i in range(TILES):
                    n = ROWS[i]
                    empty(mm, mm.first["gb"] + TILES * j + i, mix[0:n, i, j * CH:(j + 1) * CH], n, ACT.Sigmoid)
                if j == 0:
                    for i in range(TILES):
                        for half in range(2):
                            turn_hi(tp.first["ob"], 2 * i + half, ROWS[i],
                                    obT[:, 4 * half:4 * half + 4, i * P:i * P + ROWS[i]])
            split_to(S0["pb"] + 5)

            def copy_q(g):
                split_to(S0[f"q{g}"] + 3)
                for i in range(TILES):
                    n = ROWS[i]
                    empty(mm, mm.first[f"q{g}"] + i, qn[0:n, i, :], n, ACT.Copy, scale=DH ** -0.5)

            def exponentials(g, i, keys):
                nk, sc = len(keys), scs[i % 2]
                act.wait_ge(scored, 4 * g + i + 1)
                for hp in range(H):
                    ins = nc.scalar.activation(sc[:, hp, 0:nk * P], sc[:, hp, 0:nk * P], ACT.Exp,
                                               bias=oe[:, i % 2, AW + hp:AW + hp + 1],
                                               accum_out=oe[:, i % 2, AW + H + hp:AW + H + hp + 1])
                ins.then_inc(exped, 1)

            def turned(g, i, keys):
                for kk in range(len(keys)):
                    for par in range(2):
                        turn_in(tp.first[f"p{g}{i}"], 2 * kk + par, P, pT[:, kk, 4 * par:4 * par + 4, :])

            act.wait_ge(mix_out, 16 * TILES)
            copy_q(0)
            for g in range(3):
                split_to(S0[f"w{g}"] + 1)
                if g:
                    act.wait_ge(kv_out, 16 * KV_OUTS[g - 1])
                split_to(S0[f"w{g}"] + 3)
                for i in range(TILES):
                    n = ROWS[i]
                    m = mm.first[f"w{g}"] + i
                    mm.wait_filled(act, m)
                    ins = nc.scalar.activation(vn[:, i, :] if i < 4 else vs[0:NS, g, :], mm.bank(m)[0:n, :], ACT.Copy)
                    ins.then_inc(mm.done(m), 1)
                split_to(S0[f"row{2 * g + 1}"] + 1)
                for j, (dst, keep) in enumerate(((qT, qTs), (kT, kTs))):
                    for i in range(TILES):
                        turn_in(tp.first[f"qk{g}"], TILES * j + i, ROWS[i],
                                dst[:, :, i * P:(i + 1) * P] if i < 4 else keep[:, g, :, :])
                tiles = GT[4 * g:4 * g + 4]
                exponentials(*tiles[0])
                for i in range(1, 4):
                    turned(*tiles[i - 1])
                    if i == 2 and g < 2:
                        split_to(S0[f"q{g + 1}"] + 1)
                    exponentials(*tiles[i])
                if g < 2:
                    copy_q(g + 1)
                turned(*tiles[3])
            for b in range(NB + 2):
                if b == NB:
                    split_to(S0["ga"] + 1)
                if b < NB:
                    for x in range(0, XT, 2):
                        key_copy(act, nc.scalar, b, x)
                if b >= 2:
                    u = tp.first[f"ot{b - 2}"]
                    tp.wait_filled(act, u)
                    nc.scalar.activation(oT[:, :, SEQ + (b - 2) * NT:SEQ + (b - 1) * NT],
                                         tp.bank(u)[:, 0:4 * NT].rearrange("p (j n) -> p j n", j=4),
                                         ACT.Copy).then_inc(tp_act, 1)
                if b < NB:
                    act.wait_ge(s_max, b + 1)
                    for g in range(3):
                        nc.scalar.activation(ssc[0:NS, b % 2, g, :], ssc[0:NS, b % 2, g, :], ACT.Exp,
                                             bias=snm[0:NS, b % 2, g:g + 1],
                                             accum_out=sden[0:NS, b % 2, g:g + 1])
                    nc.scalar.activation(sf[0:NS, b % 2, :], sf[0:NS, b % 2, :], ACT.Exp, scale=-1.0).then_inc(s_exp, 1)
                if b < 4:
                    act.wait_ge(lse_dif, b + 1)
                    nc.scalar.activation(fw, fw, ACT.Exp, scale=-1.0).then_inc(lse_exp, 1)
                if 1 <= b <= 4:
                    turn_in(tp.first[f"o{b - 1}"], 0, P, oT[:, :, (b - 1) * P:b * P])
            for j in range(2):
                split_to(S0["ga"] + 2 * j + 3)
                for i in range(TILES):
                    n = ROWS[i]
                    empty(mm, mm.first["ga"] + TILES * j + i, sga[0:n, i, j * CH:(j + 1) * CH], n, ACT.Sigmoid)
            split_to(S0["wo"] + 3)
            for i in range(TILES):
                for half in range(2):
                    turn_hi(tp.first["mix"], 2 * i + half, ROWS[i],
                            mixT[:, 4 * half:4 * half + 4, i * P:i * P + ROWS[i]])
            split_to(S0["wo"] + 7)
            for i in range(TILES):
                n = ROWS[i]
                act.wait_ge(x1_done, i + 1)
                if i:
                    act.wait_ge(sq2, i)
                nc.scalar.activation(junk[0:n, :], x1[0:n, i, :], ACT.Square,
                                     accum_out=ss[0:n, i:i + 1]).then_inc(sq2, 1)
            act.wait_ge(var2, 1)
            nc.scalar.activation(rs, rs, ACT.Sqrt).then_inc(sqrt2, 1)
            for i in range(TILES):
                for half in range(2):
                    turn_in(tp.first["h2"], 2 * i + half, ROWS[i],
                            h2T[:, 4 * half:4 * half + 4, i * P:i * P + ROWS[i]])
            act.wait_ge(rt_exp_in, 1)
            nc.scalar.activation(eg, eg, ACT.Exp).then_inc(rt_exp, 1)
            act.wait_ge(rt_exp_in, 2)
            nc.scalar.activation(w2, w2, ACT.Exp).then_inc(rt_exp, 1)
            split_to(N_SLOTS)
            rounds = rounds_of(act)

            def high(at_, loads):
                raw, hi, _ = expert_half(at_)
                act.wait_ge(half_in[at_], loads)
                nc.scalar.activation(hi, raw, ACT.Copy).then_inc(e_hi, 1)

            def tokens_high(par, n, c):
                act.wait_ge(x_filled, n * 2 + c + 1 if n is not None else c + 1)
                nc.scalar.activation(xgT[:, par, 4 * c:4 * c + 4, :],
                                     psum[:, c, :].rearrange("p (k n) -> p k n", k=4), ACT.Copy).then_inc(x_hi, 1)

            def hidden_high(n):
                act.wait_ge(at_filled, n + 1)
                nc.scalar.activation(acT, psum[:, 4, :].rearrange("p (k n) -> p k n", k=4), ACT.Copy).then_inc(at_hi, 1)

            def silu(n):
                act.wait_ge(gate_filled, n + 1)
                nc.scalar.activation(sg, psum[:, 2, :], ACT.Silu).then_inc(sg_done, 1)

            def result(par, n, it):
                act.wait_ge(y0_filled, n + 2)
                act.wait_ge(y_out[par], it * 16 + 16)
                nc.scalar.activation(yb[:, par, 0:CH], psum[:, 5, :], ACT.Copy).then_inc(y_act, 1)

            prime(act, y_act)
            for c in range(2):
                tokens_high(0, None, c)
                high(c, 16)
            with act.Fori(0, rounds * PAIRS) as it:
                for par in range(2):
                    n = it * 2 + par
                    high(2, n * 16 + 16)
                    high(3, n * 16 + 16)
                    silu(n)
                    high(4, n * 16 + 16)
                    high(5, n * 16 + 16)
                    high(0, n * 16 + 32)
                    tokens_high(1 - par, n + 1, 0)
                    hidden_high(n)
                    tokens_high(1 - par, n + 1, 1)
                    high(1, n * 16 + 32)
                    result(par, n, it)
            for i in range(TILES):
                n = ROWS[i]
                act.wait_ge(x2_done, i + 1)
                if i:
                    act.wait_ge(sq3, i)
                nc.scalar.activation(junk_end[0:n, :], x1[0:n, i, :], ACT.Square,
                                     accum_out=ss[0:n, i:i + 1]).then_inc(sq3, 1)
                act.wait_ge(var3, i + 1)
                nc.scalar.activation(rs[0:n, i:i + 1], rs[0:n, i:i + 1], ACT.Sqrt).then_inc(sqrt3, 1)

        @block.vector
        def _(dve):
            steps = [0]

            def own(ins):
                steps[0] += 1
                ins.then_inc(dve_step, 1)
                dve.wait_ge(dve_step, steps[0])

            V = nc.vector
            parted, turned_by_act = [0], [0]

            def split_to(last):
                for n in range(parted[0], min(last + 1, N_SLOTS)):
                    if split[n]:
                        raw, hi, lo = half_slot(n)
                        dve.wait_ge(hi_done, halves_to[n])
                        V.tensor_tensor(lo, raw, hi, ALU.subtract).then_inc(lo_done, 1)
                    parted[0] = n + 1

            def turn_lo(first, u, n, hi, lo):
                turned_by_act[0] += 1
                dve.wait_ge(turned_hi, turned_by_act[0])
                V.tensor_tensor(lo, tp.bank(first + u)[:, 0:4 * n].rearrange("p (k n) -> p k n", k=4), hi,
                                ALU.subtract).then_inc(tp_dve, 1)

            def turn_tile_lo(name, i, hi, lo):
                for half in range(2):
                    ks, cols = slice(4 * half, 4 * half + 4), slice(i * P, i * P + ROWS[i])
                    turn_lo(tp.first[name], 2 * i + half, ROWS[i], hi[:, ks, cols], lo[:, ks, cols])

            V.memset(stat[:, 152:256], 1.0).then_inc(stat_set, 1)
            dve.wait_ge(stat_set, 1)
            m = tp.first["c"]
            dve.wait_ge(const_in, 16)
            tp.wait_filled(dve, m)
            own(V.tensor_copy(cT[:, :, 0:9], tp.bank(m)[:, 0:KD * 9].rearrange("p (k n) -> p k n", n=9)))
            V.tensor_tensor(cT[:, :, 9:18], tp.bank(m)[:, 0:KD * 9].rearrange("p (k n) -> p k n", n=9), cT[:, :, 0:9],
                            ALU.subtract).then_inc(tp_dve, 1)

            def modulate(name, rows, biases, base, gains, gain_n, count, targets):
                dve.wait_ge(gain_in, 16 * gain_n)

                def row(n):
                    split_to(S0[name] + min(2 * n + 3, 2 * count - 1))
                    m = row_use(name, n)
                    dve.wait_ge(bias_in[n % 2], 16 * (base + n // 2 + 1))
                    mm.wait_filled(dve, m)
                    V.tensor_tensor(rows[0:18, n % 2, :], mm.bank(m)[0:18, :], biases[0:18, n % 2, :],
                                    ALU.add).then_inc(mm_dve, 1)

                row(0)
                for n in range(count):
                    if n + 1 < count:
                        row(n + 1)
                    for s in range(2):
                        w = (P, NS)[s]
                        m = spread_use(name, n, s, count)
                        mm.wait_filled(dve, m)
                        col = slice((n % 2) * CH, (n % 2 + 1) * CH)
                        which = targets[n // 2]
                        dst = mod[0:w, which, s, col]
                        if which == 1:
                            ins = V.scalar_tensor_tensor(out=dst, in0=mm.bank(m)[0:w, :], scalar=1.0, in1=gains[0:w, col],
                                                         op0=ALU.add, op1=ALU.mult)
                        else:
                            ins = V.tensor_copy(dst, mm.bank(m)[0:w, :])
                        ins.then_inc(mm_dve, 1)

            modulate("ada1", modrow, modbias, 0, gain1, 1, 4, (0, 1))
            dve.wait_ge(sq_done, TILES)
            V.tensor_scalar(rs, ss, 1.0 / D, EPS, ALU.mult, ALU.add).then_inc(var_done, 1)
            dve.wait_ge(sqrt_done, 1)
            own(V.reciprocal(rs, rs))
            dve.wait_ge(mm_dve, 12)
            for i in range(TILES):
                n, s = ROWS[i], i // 4
                own(V.scalar_tensor_tensor(out=x0[0:n, i, :], in0=x0[0:n, i, :], scalar=rs[0:n, i:i + 1],
                                           in1=mod[0:n, 1, s, :], op0=ALU.mult, op1=ALU.mult))
                V.tensor_tensor(x0[0:n, i, :], x0[0:n, i, :], mod[0:n, 0, s, :], ALU.add).then_inc(hn_done, 1)
                if i:
                    turn_tile_lo("h", i - 1, hT, hT_lo)
            turn_tile_lo("h", TILES - 1, hT, hT_lo)
            split_to(S0["v"] + 5)
            for half in range(2):
                m = tp.first["sgu"] + half
                tp.wait_filled(dve, m)
                V.tensor_tensor(sguT[:, 4 * half:4 * half + 4, :], tp.bank(m)[:, :].rearrange("p (g n) -> p g n", g=4),
                                c_("tril").unsqueeze(1).to_broadcast([P, 4, P]), ALU.mult).then_inc(tp_dve, 1)
            m = tp.first["sgu"] + 2
            tp.wait_filled(dve, m)
            V.tensor_copy(sgubT, tp.bank(m)[:, 0:H]).then_inc(tp_dve, 1)
            split_to(S0["u"] + 3)
            for i in range(TILES):
                n = ROWS[i]
                mm.wait_emptied(dve, mm.first["v"] + TILES + i)
                for half in range(2):
                    ins = V.bn_stats(bns[0:n, i, 6 * half:6 * half + 6], mix[0:n, i, half * CH:(half + 1) * CH])
                own(ins)
                own(V.bn_aggr(mv[0:n, i, :], bns[0:n, i, :]))
                ins = V.tensor_scalar(lnr[0:n, i:i + 1], mv[0:n, i, 1:2], EPS, None, ALU.add)
            ins.then_inc(lnvar, 1)
            m = tp.first["rep"]
            tp.wait_filled(dve, m)
            V.tensor_copy(sgubTs[0:NS, :], tp.bank(m)[0:NS, NS:NS + H]).then_inc(dve_step, 1)
            steps[0] += 1
            V.tensor_tensor(sguTs[0:NS].rearrange("p g (b t) -> p g b t", b=NB),
                            tp.bank(m)[0:NS, 0:NS].rearrange("p (g t) -> p g t", g=H).unsqueeze(2).to_broadcast([NS, H, NB, NT]),
                            c_("blkt", NS).rearrange("p (b t) -> p b t", b=NB).unsqueeze(1).to_broadcast([NS, H, NB, NT]),
                            ALU.mult).then_inc(tp_dve, 1)
            dve.wait_ge(lnsqrt, 1)
            own(V.reciprocal(lnr, lnr))
            dve.wait_ge(ln_in, 32)
            for i in range(TILES):
                n = ROWS[i]
                v = mix[0:n, i, :]
                own(V.tensor_scalar(v, v, mv[0:n, i, 0:1], lnr[0:n, i:i + 1], ALU.subtract, ALU.mult))
                own(V.tensor_tensor(v, v, lng[0:n, :], ALU.mult))
                V.tensor_tensor(v, v, lnb[0:n, :], ALU.add).then_inc(vn_done, 1)
            split_to(S0["gb"] + 3)
            for i in range(TILES):
                n = ROWS[i]
                for half in range(2):
                    m = mm.first["sgu"] + 2 * i + half
                    mm.wait_filled(dve, m)
                    for k in range(4):
                        g = 4 * half + k
                        u = x0[0:n, i, g * P:(g + 1) * P]
                        b = (sgubT if i < 4 else sgubTs)[0:n, g:g + 1]
                        ins = V.scalar_tensor_tensor(out=u, in0=mm.bank(m)[0:n, k * P:(k + 1) * P], scalar=b, in1=u,
                                                     op0=ALU.add, op1=ALU.mult)
                    ins.then_inc(mm_dve, 1)
            for i in range(TILES):
                turn_tile_lo("ob", i, obT, obT_lo)
            for j in range(2):
                split_to(S0["pb"] + 2 * j + 3)
                for i in range(TILES):
                    n = ROWS[i]
                    m = mm.first["pb"] + TILES * j + i
                    x = mix[0:n, i, j * CH:(j + 1) * CH]
                    mm.wait_filled(dve, m)
                    mm.wait_emptied(dve, mm.first["gb"] + TILES * j + i)
                    V.tensor_tensor(x, mm.bank(m)[0:n, :], x, ALU.mult).then_inc(mm_dve, 1)
            def add_bias(g, i, keys):
                nk, job, sc = len(keys), 4 * g + i, scs[i % 2]
                for kk in range(nk):
                    for par in range(2):
                        m = mm.first[f"s{g}{i}"] + 2 * kk + par
                        mm.wait_filled(dve, m)
                        kind = 0 if g == 0 and nk == 2 and kk == 0 else 1
                        V.tensor_tensor(sc[:, 4 * par:4 * par + 4, kk * P:(kk + 1) * P],
                                        mm.bank(m)[:, :].rearrange("p (j n) -> p j n", j=4),
                                        abias[:, kind, 4 * par:4 * par + 4, :], ALU.add).then_inc(mm_dve, 1)
                if job >= 2:
                    dve.wait_ge(o_out[i % 2], 16 * (job // 2))
                mm.wait_emptied(dve, mm.first[f"s{g}{i}"] + 2 * nk - 1)
                V.tensor_reduce(oe[:, i % 2, AW:AW + H], sc[:, :, 0:nk * P], AX.X, ALU.max,
                                negate=True).then_inc(scored, 1)

            def copy_out(g, i):
                m = mm.first[f"o{g}{i}"]
                mm.wait_filled(dve, m)
                V.tensor_copy(oe[:, i % 2, 0:AW], mm.bank(m)[:, :]).then_inc(mm_dve, 1)

            def later_row(r):
                m, row, biases = mm.first[f"row{r}"], row_a if r < 6 else row_b, rowbias_a if r < 6 else rowbias_b
                dve.wait_ge(rowbias_in[r % 2], 16 * (r // 2 + 1))
                if r:
                    dve.wait_ge(row_out, 32 * r)
                mm.wait_filled(dve, m)
                V.tensor_tensor(row[0:9, :], mm.bank(m)[0:9, :], biases[0:9, r % 2, :], ALU.add).then_inc(mm_dve, 1)

            split_to(S0["q0"] + 3)
            dve.wait_ge(mix_out, 16 * TILES)
            for g in range(3):
                split_to(S0[f"k{g}"] + 3)
                if g:
                    dve.wait_ge(kv_out, 16 * KV_OUTS[g - 1])
                for i in range(TILES):
                    n = ROWS[i]
                    m = mm.first[f"k{g}"] + i
                    mm.wait_filled(dve, m)
                    V.tensor_copy(kn[0:n, i, :], mm.bank(m)[0:n, :]).then_inc(mm_dve, 1)
                split_to(S0[f"row{2 * g}"] + 1)
                later_row(2 * g)
                split_to(S0[f"row{2 * g + 1}"] + 1)
                dve.wait_ge(abias_in, 16 * (g + 2))
                add_bias(*GT[4 * g])
                later_row(2 * g + 1)
                for i in range(1, 4):
                    add_bias(*GT[4 * g + i])
                    if i == 2 and g < 2:
                        split_to(S0[f"q{g + 1}"] + 1)
                    if i == 3 and g < 2:
                        split_to(S0[f"k{g + 1}"] + 1)
                    copy_out(g, i - 1)
                copy_out(g, 3)

            def combine(i):
                r = oin[:, i, :].rearrange("p (g n) -> p g n", g=3)
                nm, den = r[:, :, AW:AW + H], r[:, :, AW + H:AW + 2 * H]
                own(V.tensor_reduce(nmin, nm.rearrange("p g h -> p h g"), AX.X, ALU.min))
                V.tensor_tensor(fw, nm, nmin.unsqueeze(1).to_broadcast([P, 3, H]), ALU.subtract).then_inc(lse_dif, 1)
                dve.wait_ge(lse_exp, i + 1)
                own(V.tensor_tensor(fd, fw, den, ALU.mult))
                own(V.tensor_reduce(nmin, fd.rearrange("p g h -> p h g"), AX.X, ALU.add))
                own(V.reciprocal(nmin, nmin))
                own(V.tensor_tensor(fw, fw, nmin.unsqueeze(1).to_broadcast([P, 3, H]), ALU.mult))
                for g in range(3):
                    w = fw[:, g, :].rearrange("p (par j) -> p j par", par=2).unsqueeze(3).to_broadcast([P, 4, 2, DH])
                    o = r[:, g, 0:AW].rearrange("p (j par d) -> p j par d", j=4, par=2)
                    own(V.tensor_tensor(o, o, w, ALU.mult))
                own(V.tensor_tensor(r[:, 0, 0:AW], r[:, 0, 0:AW], r[:, 1, 0:AW], ALU.add))
                V.tensor_tensor(r[:, 0, 0:AW], r[:, 0, 0:AW], r[:, 2, 0:AW], ALU.add).then_inc(oc_done, 1)

            def spread_q(b):
                if b >= 2:
                    mm.wait_filled(dve, mm.first[f"ss{b - 2}"] + 2)
                for half in range(2):
                    r = slice(64 * half, 64 * half + 64)
                    blocks = Qm[r, b % 2, :]

                    def spread(block, count):
                        a = block * 256 + half
                        return blocks[:, a:a + 66 * count].rearrange("p (n x) -> p n x", x=66)

                    for g, block in ((0, 0), (1, 13), (2, 14)):
                        V.tensor_copy(spread(block, 4)[:, :, 0:64].rearrange("p j (t y) -> p j t y", y=8)[:, :, :, 0],
                                      qTs[r, g, :, b * NT:(b + 1) * NT])
                    V.tensor_copy(spread(1, 16)[:, :, 0:64].rearrange("p (r j) (u y) -> p r j u y", j=4, y=32)[:, :, :, :, 0],
                                  qTs[r, 1, :, b * NT:(b + 1) * NT].rearrange("p j (u r) -> p r j u", r=4))
                    ins = V.tensor_copy(spread(5, 32)[:, :, 0].rearrange("p (t j) -> p t j", j=4),
                                        qTs[r, 2, :, b * NT:(b + 1) * NT].rearrange("p j t -> p t j"))
                ins.then_inc(q_spread, 1)

            key_copy = copy_keys(tp, KT, kt_read)
            own(V.memset(pTm, 0.0))
            tp.wait_emptied(dve, tp.first["qk2"] + 2 * TILES - 1)
            own(V.memset(Qm[:, 0, :], 0.0))
            spread_q(0)
            for b in range(NB + 1):
                if b == NB:
                    split_to(S0["ga"] + 1)
                if b < NB:
                    for x in range(1, XT, 2):
                        key_copy(dve, V, b, x)
                    dve.wait_ge(sb_in[b % 2], 16 * (b // 2 + 1))
                    for g in range(3):
                        m = mm.first[f"ss{b}"] + g
                        mm.wait_filled(dve, m)
                        if b >= 2 and g == 0:
                            tp.wait_filled(dve, tp.first[f"pt{b - 2}"])
                        V.tensor_tensor(ssc[0:NS, b % 2, g, :], mm.bank(m)[0:NS, 0:KEYS], sbias[0:NS, b % 2, g, :],
                                        ALU.add).then_inc(mm_dve, 1)
                    mm.wait_emptied(dve, mm.first[f"ss{b}"] + 2)
                    nm = snm[0:NS, b % 2, :]
                    own(V.tensor_reduce(nm, ssc[0:NS, b % 2, :, :], AX.X, ALU.max, negate=True))
                    own(V.tensor_reduce(smin[0:NS, 0:1], nm, AX.X, ALU.min))
                    V.tensor_scalar(sf[0:NS, b % 2, :], nm, smin[0:NS, 0:1], None, ALU.subtract).then_inc(s_max, 1)
                    if b == 0:
                        dve.wait_ge(q_zero, 1)
                    if b + 1 < NB:
                        spread_q(b + 1)
                if b >= 1:
                    c, f = b - 1, sf[0:NS, (b - 1) % 2, :]
                    u = tp.first[f"pt{c}"]
                    tp.wait_filled(dve, u)
                    if c:
                        mm.wait_filled(dve, mm.first[f"so{c - 1}"])
                    bank = tp.bank(u)
                    V.tensor_copy(pTn[0:NS, :, :], bank[0:NS, 3 * NS:6 * NS].rearrange("p (g n) -> p g n", g=3))
                    V.tensor_copy(pTm[:, 0:NS], bank[:, 0:NS])
                    for v in range(2):
                        V.tensor_copy(pTm[:, NS + 32 * v:NS + 32 * v + 288].rearrange("p (r x) -> p r x", x=72)[:, :, 0:H],
                                      bank[:, NS + 32 * v:NS + 32 * v + 32].rearrange("p (r h) -> p r h", h=H))
                    V.tensor_copy(pTm[:, 5 * NS:5 * NS + 576].rearrange("p (t x) -> p t x", x=72)[:, :, 0:H],
                                  bank[:, 2 * NS:3 * NS].rearrange("p (t h) -> p t h", h=H)).then_inc(tp_dve, 1)
                    m = mm.first[f"so{c}"]
                    mm.wait_filled(dve, m)
                    if c:
                        tp.wait_filled(dve, tp.first[f"ot{c - 1}"])
                    V.tensor_tensor(om[0:NS, :], mm.bank(m)[0:NS, :], c_("dmask", NS), ALU.mult).then_inc(mm_dve, 1)
                if b < NB:
                    f, d = sf[0:NS, b % 2, :], sden[0:NS, b % 2, :]
                    dve.wait_ge(s_exp, b + 1)
                    own(V.tensor_tensor(d, d, f, ALU.mult))
                    own(V.tensor_reduce(smin[0:NS, 1:2], d, AX.X, ALU.add))
                    own(V.reciprocal(smin[0:NS, 1:2], smin[0:NS, 1:2]))
                    own(V.tensor_scalar(f, f, smin[0:NS, 1:2], None, ALU.mult))
                    V.tensor_tensor(ssc[0:NS, b % 2, :, :], ssc[0:NS, b % 2, :, :],
                                    f.unsqueeze(2).to_broadcast([NS, 3, KEYS]), ALU.mult).then_inc(p_ready, 1)
                if b < 4:
                    if b == 0:
                        dve.wait_ge(oin_in, 48)
                    combine(b)
            split_to(S0["pa"] + 3)
            dve.wait_ge(mix_back, 32)
            for c in range(2):
                for i in range(TILES):
                    n = ROWS[i]
                    m = mm.first["pa"] + TILES * c + i
                    s_, x = sga[0:n, i, c * CH:(c + 1) * CH], mix[0:n, i, c * CH:(c + 1) * CH]
                    mm.wait_filled(dve, m)
                    mm.wait_emptied(dve, mm.first["ga"] + TILES * c + i)
                    own(V.tensor_tensor(s_, mm.bank(m)[0:n, :], s_, ALU.mult))
                    V.tensor_tensor(x, x, s_, ALU.add).then_inc(mm_dve, 1)


            def scale_gain(norm):
                dve.wait_ge(gain_in, 16 * (norm + 2))
                dve.wait_ge(mod_in, 16 * 6 * (norm + 1))
                for s in range(2):
                    w = (P, NS)[s]
                    m = mod[0:w, 1, s, :]
                    own(V.scalar_tensor_tensor(out=m, in0=m, scalar=1.0, in1=gain[0:w, :], op0=ALU.add, op1=ALU.mult))
                V.sem_inc(gain_used, 1)

            for i in range(TILES):
                turn_tile_lo("mix", i, mixT, mixT_lo)
            dve.wait_ge(x1_in, 32)
            scale_gain(0)
            for j in range(2):
                split_to(S0["wo"] + 2 * j + 3)
                for i in range(TILES):
                    n, s = ROWS[i], i // 4
                    m = mm.first["wo"] + TILES * j + i
                    x = x1[0:n, i, j * CH:(j + 1) * CH]
                    mm.wait_filled(dve, m)
                    if j and i:
                        dve.wait_ge(x1_done, i)
                    V.tensor_tensor(gt_tmp[0:n, :], mm.bank(m)[0:n, :], mod[0:n, 2, s, j * CH:(j + 1) * CH],
                                    ALU.mult).then_inc(mm_dve, 1)
                    mm.wait_emptied(dve, m)
                    ins = V.tensor_tensor(x, x, gt_tmp[0:n, :], ALU.add)
                    if j:
                        ins.then_inc(x1_done, 1)
                    else:
                        own(ins)
            dve.wait_ge(sq2, TILES)
            V.tensor_scalar(rs, ss, 1.0 / D, EPS, ALU.mult, ALU.add).then_inc(var2, 1)
            dve.wait_ge(sqrt2, 1)
            own(V.reciprocal(rs, rs))
            for i in range(TILES):
                n, s = ROWS[i], i // 4
                if i >= 2:
                    dve.wait_ge(h2_out[i % 2], 16 * (i // 2))
                    tp.wait_filled(dve, tp.first["h2"] + 2 * (i - 2) + 1)
                own(V.scalar_tensor_tensor(out=hrow[0:n, i % 2, :], in0=x1[0:n, i, :], scalar=rs[0:n, i:i + 1],
                                           in1=mod[0:n, 1, s, :], op0=ALU.mult, op1=ALU.mult))
                V.tensor_tensor(hrow[0:n, i % 2, :], hrow[0:n, i % 2, :], mod[0:n, 0, s, :], ALU.add).then_inc(h2_done, 1)
            split_to(S0["wo"] + 7)
            own(V.memset(rt(0, 780), 0.0))
            dve.wait_ge(rt_in, 16 * 7)
            for i in range(TILES):
                n = ROWS[i]
                m = mm.first["rt"] + i
                mm.wait_filled(dve, m)
                V.tensor_tensor(lg[0:n, i, :], mm.bank(m)[0:n, 0:20], brt[0:n, :], ALU.add).then_inc(mm_dve, 1)
            mm.wait_emptied(dve, mm.first["rt"] + TILES - 1)
            iota4 = c_("iota")[:, 0:4].unsqueeze(1).to_broadcast([P, TILES, 4])

            def wide(a):
                return a.unsqueeze(2).to_broadcast([P, TILES, 4])

            def first_best(values, best, onehot):
                own(V.tensor_reduce(best, values, AX.X, ALU.max))
                own(V.tensor_tensor(eq4, values, wide(best), ALU.is_equal))
                own(V.scalar_tensor_tensor(out=cand4, in0=eq4, scalar=-99.0, in1=iota4, op0=ALU.mult, op1=ALU.add))
                own(V.tensor_reduce(id5, cand4, AX.X, ALU.min))
                own(V.tensor_scalar(id5, id5, 99.0, None, ALU.add))
                own(V.tensor_tensor(onehot, iota4, wide(id5), ALU.is_equal))

            first_best(lg[:, :, 0:4], sc5, on_g)
            V.tensor_tensor(eg, lg[:, :, 0:4], wide(sc5), ALU.subtract).then_inc(rt_exp_in, 1)
            own(V.tensor_tensor(tmp5, lg[:, :, 4:20].rearrange("p i (g e) -> p i g e", g=4),
                                on_g.unsqueeze(3).to_broadcast([P, TILES, 4, 4]), ALU.mult))
            own(V.tensor_reduce(esel, tmp5.rearrange("p i g e -> p i e g"), AX.X, ALU.add))
            first_best(esel, e1m, on_1)
            own(V.scalar_tensor_tensor(out=esel2, in0=on_1, scalar=NEG, in1=esel, op0=ALU.mult, op1=ALU.add))
            first_best(esel2, e2m, on_2)
            dve.wait_ge(rt_exp, 1)
            own(V.tensor_reduce(gp, eg, AX.X, ALU.add))
            own(V.reciprocal(gp, gp))
            V.tensor_tensor(w2, e2m, e1m, ALU.subtract).then_inc(rt_exp_in, 1)
            for on, mk in ((on_1, m1), (on_2, m2)):
                own(V.tensor_tensor(mk.rearrange("p i (g e) -> p i g e", g=4),
                                    on_g.unsqueeze(3).to_broadcast([P, TILES, 4, 4]),
                                    on.unsqueeze(2).to_broadcast([P, TILES, 4, 4]), ALU.mult))
            own(V.tensor_tensor(mask, m1, m2, ALU.add))
            V.tensor_tensor(mask, mask, c_("valid").unsqueeze(2).to_broadcast([P, TILES, 16]), ALU.mult).then_inc(mask_done, 1)
            dve.wait_ge(rt_exp, 2)
            own(V.tensor_scalar(w1, w2, 1.0, None, ALU.add))
            own(V.reciprocal(w1, w1))
            own(V.tensor_tensor(w1, w1, gp, ALU.mult))
            own(V.tensor_tensor(w2, w2, w1, ALU.mult))
            m = tp.first["pos"]
            tp.wait_filled(dve, m)
            own(V.tensor_tensor(place, tp.bank(m)[:, 0:80].rearrange("p (i e) -> p i e", e=16),
                                c_("ebase").unsqueeze(1).to_broadcast([P, TILES, 16]), ALU.add))
            own(V.tensor_reduce(rounds_f, tp.bank(m)[:, 80:96], AX.X, ALU.max))
            own(V.tensor_scalar(sc5, c_("iota")[:, 0:TILES], float(CAP), rounds_f, ALU.mult, ALU.is_lt))
            own(V.tensor_reduce(rounds_f, sc5, AX.X, ALU.add))
            own(V.tensor_scalar(rounds_f, rounds_f, 1.0, None, ALU.max))
            V.tensor_copy(rounds_u, rounds_f).then_inc(tp_dve, 1)
            for k, mk in enumerate((m1, m2)):
                own(V.tensor_tensor(pick, place, mk, ALU.mult))
                own(V.tensor_reduce(rowf[:, k, :], pick, AX.X, ALU.add))
            V.tensor_copy(row_u, rowf).then_inc(rows_done, 1)
            later_row(6)
            split_to(S0["row8"] + 1)
            later_row(7)
            for r in range(8, 12):
                if r < 11:
                    split_to(S0[f"row{r + 1}"] + 1)
                later_row(r)
            rounds = rounds_of(dve)

            def low(at_, made):
                raw, hi, lo = expert_half(at_)
                dve.wait_ge(e_hi, made)
                V.tensor_tensor(lo, raw, hi, ALU.subtract).then_inc(e_lo, 1)

            def tokens_low(par, n, c):
                dve.wait_ge(x_hi, n * 2 + c + 1 if n is not None else c + 1)
                V.tensor_tensor(xgT_lo[:, par, 4 * c:4 * c + 4, :], psum[:, c, :].rearrange("p (k n) -> p k n", k=4),
                                xgT[:, par, 4 * c:4 * c + 4, :], ALU.subtract).then_inc(x_lo, 1)

            def hidden_low(n):
                dve.wait_ge(at_hi, n + 1)
                V.tensor_tensor(acT_lo, psum[:, 4, :].rearrange("p (k n) -> p k n", k=4), acT,
                                ALU.subtract).then_inc(at_lo, 1)

            def gated(n):
                dve.wait_ge(up_filled, n + 2)
                dve.wait_ge(sg_done, n + 1)
                V.tensor_tensor(ac, psum[:, 3, :], sg, ALU.mult).then_inc(ac_done, 1)

            def result(par, n, it):
                dve.wait_ge(y1_filled, n + 2)
                dve.wait_ge(y_out[par], it * 16 + 16)
                V.tensor_copy(yb[:, par, CH:D], psum[:, 6, :]).then_inc(y_dve, 1)

            prime(dve, y_dve)
            for c in range(2):
                tokens_low(0, None, c)
                low(c, c + 1)
            with dve.Fori(0, rounds * PAIRS) as it:
                for par in range(2):
                    n = it * 2 + par
                    low(2, n * 6 + 3)
                    low(3, n * 6 + 4)
                    low(4, n * 6 + 5)
                    gated(n)
                    tokens_low(1 - par, n + 1, 0)
                    hidden_low(n)
                    tokens_low(1 - par, n + 1, 1)
                    low(5, n * 6 + 6)
                    low(0, n * 6 + 7)
                    low(1, n * 6 + 8)
                    result(par, n, it)
            scale_gain(1)
            for i in range(TILES):
                n, s = ROWS[i], i // 4
                y1, y2 = yg[0:n, i % 2, 0, :], yg[0:n, i % 2, 1, :]
                x = x1[0:n, i, :]
                dve.wait_ge(yg_in2[i % 2], 16 * (i // 2 + 1))
                own(V.tensor_scalar(y1, y1, w1[0:n, i:i + 1], None, ALU.mult))
                own(V.scalar_tensor_tensor(out=y1, in0=y2, scalar=w2[0:n, i:i + 1], in1=y1, op0=ALU.mult, op1=ALU.add))
                own(V.tensor_tensor(y1, y1, mod[0:n, 2, s, :], ALU.mult))
                V.tensor_tensor(x, x, y1, ALU.add).then_inc(x2_done, 1)
                dve.wait_ge(sq3, i + 1)
                V.tensor_scalar(rs[0:n, i:i + 1], ss[0:n, i:i + 1], 1.0 / D, EPS, ALU.mult, ALU.add).then_inc(var3, 1)
                dve.wait_ge(sqrt3, i + 1)
                own(V.reciprocal(rs[0:n, i:i + 1], rs[0:n, i:i + 1]))
                own(V.scalar_tensor_tensor(out=x, in0=x, scalar=rs[0:n, i:i + 1], in1=mod[0:n, 1, s, :],
                                           op0=ALU.mult, op1=ALU.mult))
                V.tensor_tensor(x, x, mod[0:n, 0, s, :], ALU.add).then_inc(y_done, 1)


_INS = ["x_prompt", "x_sample", "cache_kv_w128", "cache_kv_w512", "cache_kv_w2048", "c_prompt", "c_sample", "w_ada",
        "b_ada", "norm1_g", "norm2_g", "w_in", "sgu_ln_g", "sgu_ln_b", "sgu_w", "sgu_b", "w_pa", "w_pb", "w_o",
        "w_route_group", "b_route_group", "w_route_expert", "b_route_expert", "w_gate", "w_up", "w_down", "normf_g",
        "w_ada_final", "b_ada_final"]
_OUTS = [(1, SEQ, D), (NB, NT, D)] + [(1, 1, min(w, SEQ), 2, H, DH) for w in WINS] + [(1, NB, NT, 2, H, DH)] * 3 + [
    (1, NB, NT, D)]


def kernel(**inputs):
    import numpy as _np
    import concourse.bacc as _bacc
    from concourse import mybir as _mybir
    from concourse.bass_utils import run_bass_kernel_spmd as _run

    nc = _bacc.Bacc("TRN2", target_bir_lowering=False, num_devices=1)
    arrays, t = {}, {}
    given = {name: _np.ascontiguousarray(inputs[name]) for name in _INS}
    given |= {"consts": constants(), "pbias": prompt_bias(), "sbias": sample_bias(),
              "empty_slots": empty_slots(), "token_places": token_places()}
    for name, a in given.items():
        arrays[f"in_{name}_dram"] = a
        t[name] = nc.dram_tensor(f"in_{name}_dram", a.shape, _mybir.dt.from_np(a.dtype), kind="ExternalInput").ap()
    outs = [nc.dram_tensor(f"out_{i}_dram", s, _mybir.dt.float32, kind="ExternalOutput").ap() for i, s in enumerate(_OUTS)]
    named = {"y_prompt": outs[0][0], "y_sample": outs[1].rearrange("b t d -> (b t) d"),
             "kvp": [o[0, 0].rearrange("s c h d -> s (c h d)") for o in outs[2:5]],
             "kvs": [o[0].rearrange("b t c h d -> (b t) (c h d)") for o in outs[5:8]],
             "sgu_v": outs[8][0].rearrange("b t d -> (b t) d")}
    build(nc, t, named)
    r = _run(nc, [arrays], core_ids=[0])
    return tuple(r.results[0][f"out_{i}_dram"] for i in range(len(_OUTS)))
```
